# Optimizing a Trainium2 kernel written in Bass

```python
import jax, jax.numpy as jnp
from jax import lax
import numpy as np

D_MODEL = 1024
BATCH = 1
SEQ = 256
DEPTH = 2

PLE_DIM = 256
MLA_HEADS = 8
MLA_NOPE = 64
MLA_ROPE = 32
MLA_V = 64
MLA_QK = MLA_NOPE + MLA_ROPE
MLA_Q_LORA = 384
MLA_KV_LORA = 128
ROPE_THETA = 10000.0
Q_BLOCK = 128
FNET_GROUPS = 4
GQA_Q_HEADS = 8
GQA_KV_HEADS = 2
GQA_GROUP = GQA_Q_HEADS // GQA_KV_HEADS
GQA_HEAD_DIM = 64
WINDOW = 128
WIN_BLOCK = 128
FFN_DIM = -(-8 * D_MODEL // (3 * 256)) * 256
RMS_EPS = 1e-6

IN_SPLITS = (MLA_Q_LORA, MLA_KV_LORA, MLA_ROPE,
             GQA_Q_HEADS * GQA_HEAD_DIM, GQA_KV_HEADS * GQA_HEAD_DIM, GQA_KV_HEADS * GQA_HEAD_DIM,
             D_MODEL, D_MODEL, D_MODEL)
IN_COLS = sum(IN_SPLITS)


def rms_norm(x, gain):
    xf = x.astype(jnp.float32)
    y = xf * lax.rsqrt(jnp.mean(xf * xf, axis=-1, keepdims=True) + RMS_EPS)
    return (y * gain.astype(jnp.float32)).astype(x.dtype)

def apply_rope(t, positions):
    half = t.shape[-1] // 2
    inv_freq = ROPE_THETA ** (-jnp.arange(half, dtype=jnp.float32) / half)
    ang = positions.astype(jnp.float32)[..., None] * inv_freq
    ang = ang.reshape(ang.shape[:2] + (1,) * (t.ndim - 3) + (half,))
    cos, sin = jnp.cos(ang), jnp.sin(ang)
    tf = t.astype(jnp.float32)
    t1, t2 = tf[..., :half], tf[..., half:]
    return jnp.concatenate([t1 * cos - t2 * sin, t1 * sin + t2 * cos], axis=-1).astype(t.dtype)

def alibi_slopes(n_heads):
    return 2.0 ** (-8.0 * (np.arange(n_heads, dtype=np.float32) + 1.0) / n_heads)

def mla_attention(c_q, c_kv, k_rope, positions, q_norm, w_uq, kv_norm, w_ukv):
    B, S, _ = c_q.shape
    q = (rms_norm(c_q, q_norm) @ w_uq).reshape(B, S, MLA_HEADS, MLA_QK)
    q_nope = q[..., :MLA_NOPE]
    q_rope = apply_rope(q[..., MLA_NOPE:], positions)
    kv = (rms_norm(c_kv, kv_norm) @ w_ukv).reshape(B, S, MLA_HEADS, MLA_NOPE + MLA_V)
    k_nope, v = kv[..., :MLA_NOPE], kv[..., MLA_NOPE:]
    k_r = apply_rope(k_rope, positions)
    scale = MLA_QK ** -0.5
    nb = S // Q_BLOCK
    qn_b = q_nope.reshape(B, nb, Q_BLOCK, MLA_HEADS, MLA_NOPE).transpose(1, 0, 2, 3, 4)
    qr_b = q_rope.reshape(B, nb, Q_BLOCK, MLA_HEADS, MLA_ROPE).transpose(1, 0, 2, 3, 4)

    def attend(blk):
        qn, qr = blk
        s = (jnp.einsum('bqhd,bkhd->bhqk', qn, k_nope)
             + jnp.einsum('bqhr,bkr->bhqk', qr, k_r)).astype(jnp.float32) * scale
        probs = jax.nn.softmax(s, axis=-1).astype(v.dtype)
        return jnp.einsum('bhqk,bkhd->bqhd', probs, v)

    o = lax.map(attend, (qn_b, qr_b))
    return o.transpose(1, 0, 2, 3, 4).reshape(B, S, MLA_HEADS * MLA_V)

def fourier_mix(h):
    B, S, D = h.shape
    hg = h.astype(jnp.float32).reshape(B, S, FNET_GROUPS, D // FNET_GROUPS)
    f = jnp.fft.fftn(hg, axes=(1, 3), norm='ortho').real
    return f.reshape(B, S, D).astype(h.dtype)

def windowed_gqa(q, k, v, positions, sink):
    B, S, _ = q.shape
    nb = S // WIN_BLOCK
    q = q.reshape(B, nb, WIN_BLOCK, GQA_KV_HEADS, GQA_GROUP, GQA_HEAD_DIM)
    k = k.reshape(B, S, GQA_KV_HEADS, GQA_HEAD_DIM)
    v = v.reshape(B, S, GQA_KV_HEADS, GQA_HEAD_DIM)

    def windows(t):
        pad = ((0, 0), (WIN_BLOCK, WIN_BLOCK)) + ((0, 0),) * (t.ndim - 2)
        tb = jnp.pad(t, pad).reshape((B, nb + 2, WIN_BLOCK) + t.shape[2:])
        return jnp.concatenate([tb[:, :-2], tb[:, 1:-1], tb[:, 2:]], axis=2)

    kw, vw, pw = windows(k), windows(v), windows(positions)
    scale = GQA_HEAD_DIM ** -0.5
    s = jnp.einsum('bnqhgd,bnkhd->bnhgqk', q, kw).astype(jnp.float32) * scale
    pq = positions.reshape(B, nb, WIN_BLOCK)
    dist = jnp.abs(pq[..., :, None] - pw[..., None, :]).astype(jnp.float32)
    slopes = jnp.asarray(alibi_slopes(GQA_Q_HEADS)).reshape(GQA_KV_HEADS, GQA_GROUP)
    s = s - slopes[None, None, :, :, None, None] * dist[:, :, None, None]
    qi = jnp.arange(WIN_BLOCK)
    kj = jnp.arange(3 * WIN_BLOCK)
    band = jnp.abs(kj[None, :] - WIN_BLOCK - qi[:, None]) <= WINDOW
    key_idx = jnp.arange(nb)[:, None] * WIN_BLOCK - WIN_BLOCK + kj[None, :]
    valid = (key_idx >= 0) & (key_idx < S)
    mask = band[None] & valid[:, None, :]
    s = jnp.where(mask[None, :, None, None], s, -jnp.inf)
    sink_l = sink.astype(jnp.float32).reshape(GQA_KV_HEADS, GQA_GROUP)[None, None, :, :, None, None]
    m = jnp.maximum(jnp.max(s, axis=-1, keepdims=True), sink_l)
    e = jnp.exp(s - m)
    probs = (e / (jnp.sum(e, axis=-1, keepdims=True) + jnp.exp(sink_l - m))).astype(v.dtype)
    o = jnp.einsum('bnhgqk,bnkhd->bnqhgd', probs, vw)
    return o.reshape(B, S, GQA_Q_HEADS * GQA_HEAD_DIM)

def first_inputs(seed: int = 0) -> dict:
    key = jax.random.key(seed)
    ks = iter(jax.random.split(key, 32))

    def w(shape, fan_in):
        return jax.random.normal(next(ks), shape, jnp.float32) * (fan_in ** -0.5)

    def gain(n):
        return 1.0 + 0.1 * jax.random.normal(next(ks), (DEPTH, n), jnp.float32)

    x = jax.random.normal(next(ks), (BATCH, SEQ, D_MODEL), jnp.float32)
    p = jax.random.normal(next(ks), (DEPTH, BATCH, SEQ, PLE_DIM), jnp.float32)
    offset = jax.random.randint(next(ks), (BATCH, 1), 0, 4096, jnp.int32)
    positions = (offset + jnp.arange(SEQ, dtype=jnp.int32)[None, :]).astype(jnp.int32)
    return {
        'x': x,
        'p': p,
        'positions': positions,
        'norm_mix_pre': gain(D_MODEL),
        'w_in': w((DEPTH, D_MODEL, IN_COLS), D_MODEL),
        'mla_q_norm': gain(MLA_Q_LORA),
        'w_uq': w((DEPTH, MLA_Q_LORA, MLA_HEADS * MLA_QK), MLA_Q_LORA),
        'mla_kv_norm': gain(MLA_KV_LORA),
        'w_ukv': w((DEPTH, MLA_KV_LORA, MLA_HEADS * (MLA_NOPE + MLA_V)), MLA_KV_LORA),
        'gqa_sink': 0.5 * jax.random.normal(next(ks), (DEPTH, GQA_Q_HEADS), jnp.float32),
        'w_branch_a': w((DEPTH, MLA_HEADS * MLA_V, D_MODEL), MLA_HEADS * MLA_V),
        'w_branch_b': w((DEPTH, D_MODEL, D_MODEL), D_MODEL),
        'w_branch_c': w((DEPTH, GQA_Q_HEADS * GQA_HEAD_DIM, D_MODEL), GQA_Q_HEADS * GQA_HEAD_DIM),
        'w_out': w((DEPTH, D_MODEL, D_MODEL), D_MODEL),
        'norm_mix_post': gain(D_MODEL),
        'norm_ffn_pre': gain(D_MODEL),
        'w_ffn_gate': w((DEPTH, D_MODEL, FFN_DIM), D_MODEL),
        'w_ffn_up': w((DEPTH, D_MODEL, FFN_DIM), D_MODEL),
        'w_ffn_down': w((DEPTH, FFN_DIM, D_MODEL), FFN_DIM),
        'norm_ffn_post': gain(D_MODEL),
        'w_ple_proj': w((DEPTH, PLE_DIM, D_MODEL), PLE_DIM),
        'w_ple_gate': w((DEPTH, D_MODEL, D_MODEL), D_MODEL),
        'norm_ple': gain(D_MODEL),
    }

def first_block(x, p, positions, norm_mix_pre, w_in, mla_q_norm, w_uq, mla_kv_norm, w_ukv,
              gqa_sink, w_branch_a, w_branch_b, w_branch_c, w_out, norm_mix_post,
              norm_ffn_pre, w_ffn_gate, w_ffn_up, w_ffn_down, norm_ffn_post,
              w_ple_proj, w_ple_gate, norm_ple):
    split_points = list(np.cumsum(IN_SPLITS)[:-1])
    for i in range(DEPTH):
        h = rms_norm(x, norm_mix_pre[i])
        z = h @ w_in[i]
        c_q, c_kv, k_rope, q_c, k_c, v_c, g_a, g_b, g_c = jnp.split(z, split_points, axis=-1)
        o_a = mla_attention(c_q, c_kv, k_rope, positions, mla_q_norm[i], w_uq[i],
                            mla_kv_norm[i], w_ukv[i])
        o_b = fourier_mix(h)
        o_c = windowed_gqa(q_c, k_c, v_c, positions, gqa_sink[i])
        merged = (jax.nn.sigmoid(g_a) * (o_a @ w_branch_a[i])
                  + jax.nn.sigmoid(g_b) * (o_b @ w_branch_b[i])
                  + jax.nn.sigmoid(g_c) * (o_c @ w_branch_c[i]))
        x = x + rms_norm(merged @ w_out[i], norm_mix_post[i])
        h = rms_norm(x, norm_ffn_pre[i])
        ff = (jax.nn.silu(h @ w_ffn_gate[i]) * (h @ w_ffn_up[i])) @ w_ffn_down[i]
        x = x + rms_norm(ff, norm_ffn_post[i])
        e = (p[i] @ w_ple_proj[i]) * jax.nn.sigmoid(x @ w_ple_gate[i])
        x = x + rms_norm(e, norm_ple[i])
    return x


N_HEADS = 16
HEAD_DIM = 64
ATTN_DIM = N_HEADS * HEAD_DIM
ROT_DIM = HEAD_DIM // 4
ROPE_THETA_2 = 500000.0
D_FF = 2816
FFN_RESIDUAL_WEIGHT = 0.5
N_A_LAYERS = DEPTH // 2
N_B_LAYERS = DEPTH - N_A_LAYERS
DILATION_PAIRS = ((128, 1), (512, 4), (2048, 16))
MOBA_BLOCK = 256
MOBA_TOPK = 3
MOBA_Q_CHUNK = 32


def rmsnorm(x, g):
    xf = x.astype(jnp.float32)
    y = xf * lax.rsqrt(jnp.mean(xf * xf, axis=-1, keepdims=True) + RMS_EPS)
    return (y * g.astype(jnp.float32)).astype(x.dtype)

def swiglu(h, w_gate, w_up, w_down):
    return (jax.nn.silu(h @ w_gate) * (h @ w_up)) @ w_down

def partial_rotary(t, pos):
    half = ROT_DIM // 2
    inv_freq = ROPE_THETA_2 ** (-jnp.arange(half, dtype=jnp.float32) / half)
    ang = pos.astype(jnp.float32)[:, None] * inv_freq[None, :]
    cos, sin = jnp.cos(ang), jnp.sin(ang)
    tf = t.astype(jnp.float32)
    x1, x2 = tf[..., :half], tf[..., half:ROT_DIM]
    out = jnp.concatenate([x1 * cos - x2 * sin, x1 * sin + x2 * cos, tf[..., ROT_DIM:]], axis=-1)
    return out.astype(t.dtype)

def dilated_branch(q, k, v, window, dil):
    B, H, S, Dh = q.shape
    blk = window // dil
    span = blk * dil
    s_pad = -(-S // span) * span
    L = s_pad // dil
    nb = L // blk

    def to_sub(t):
        t = jnp.pad(t, ((0, 0), (0, 0), (0, s_pad - S), (0, 0)))
        t = t.reshape(B, H, L, dil, Dh).transpose(0, 1, 3, 2, 4)
        return t.reshape(B, H, dil, nb, blk, Dh)

    qs, ks, vs = to_sub(q), to_sub(k), to_sub(v)

    def with_prev(t):
        prev = jnp.pad(t, ((0, 0), (0, 0), (0, 0), (1, 0), (0, 0), (0, 0)))[:, :, :, :-1]
        return jnp.concatenate([prev, t], axis=4)

    kk, vv = with_prev(ks), with_prev(vs)
    s = jnp.einsum('bhrnqd,bhrnkd->bhrnqk', qs, kk).astype(jnp.float32) * (HEAD_DIM ** -0.5)
    qi = jnp.arange(blk)[:, None]
    kj = jnp.arange(2 * blk)[None, :]
    diff = blk + qi - kj
    band = (diff >= 0) & (diff <= blk)
    has_prev = (jnp.arange(nb)[:, None, None] > 0) | (kj[None] >= blk)
    mask = band[None] & has_prev
    s = jnp.where(mask, s, -jnp.inf)
    m = jnp.max(s, axis=-1, keepdims=True)
    p = jnp.exp(s - m)
    l = jnp.sum(p, axis=-1, keepdims=True)
    o = jnp.einsum('bhrnqk,bhrnkd->bhrnqd', (p / l).astype(v.dtype), vv)
    lse = m + jnp.log(l)

    def from_sub(t):
        X = t.shape[-1]
        t = t.reshape(B, H, dil, L, X).transpose(0, 1, 3, 2, 4).reshape(B, H, s_pad, X)
        return t[:, :, :S]

    return from_sub(o), from_sub(lse)[..., 0]

def mixer_a(h, w_qkv, w_o, pos):
    B, S, _ = h.shape
    qkv = (h @ w_qkv).reshape(B, S, 3, N_HEADS, HEAD_DIM).transpose(2, 0, 3, 1, 4)
    q, k, v = partial_rotary(qkv[0], pos), partial_rotary(qkv[1], pos), qkv[2]
    outs, lses = [], []
    for window, dil in DILATION_PAIRS:
        o_i, lse_i = dilated_branch(q, k, v, window, dil)
        outs.append(o_i)
        lses.append(lse_i)
    wts = jax.nn.softmax(jnp.stack(lses, axis=0), axis=0)
    o = jnp.sum(wts[..., None] * jnp.stack(outs, axis=0).astype(jnp.float32), axis=0).astype(h.dtype)
    return o.transpose(0, 2, 1, 3).reshape(B, S, ATTN_DIM) @ w_o

def shared_kv(h_stream, kv_norm, kv_w, pos):
    B, S, _ = h_stream.shape
    hn = rmsnorm(h_stream, kv_norm)
    kv = (hn @ kv_w).reshape(B, S, 2, N_HEADS, HEAD_DIM).transpose(2, 0, 3, 1, 4)
    k, v = partial_rotary(kv[0], pos), kv[1]
    s_pad = -(-S // MOBA_BLOCK) * MOBA_BLOCK
    pad = ((0, 0), (0, 0), (0, s_pad - S), (0, 0))
    k_pad, v_pad = jnp.pad(k, pad), jnp.pad(v, pad)
    nb = s_pad // MOBA_BLOCK
    k_mean = jnp.mean(k_pad.reshape(B, N_HEADS, nb, MOBA_BLOCK, HEAD_DIM).astype(jnp.float32), axis=3)
    return k_pad, v_pad, k_mean.astype(k.dtype)

def mixer_b(h, w_q, w_o, k_pad, v_pad, k_mean, pos):
    B, S, _ = h.shape
    q = (h @ w_q).reshape(B, S, N_HEADS, HEAD_DIM).transpose(0, 2, 1, 3)
    q = partial_rotary(q, pos)
    nb = k_mean.shape[2]
    ksel = min(MOBA_TOPK, nb)
    k_blocks = k_pad.reshape(B, N_HEADS, nb, MOBA_BLOCK, HEAD_DIM)
    v_blocks = v_pad.reshape(B, N_HEADS, nb, MOBA_BLOCK, HEAD_DIM)
    n_chunks = S // MOBA_Q_CHUNK
    q_chunks = q.reshape(B, N_HEADS, n_chunks, MOBA_Q_CHUNK, HEAD_DIM).transpose(2, 0, 1, 3, 4)
    gather = jax.vmap(jax.vmap(lambda blocks, idx: blocks[idx]))
    scale = HEAD_DIM ** -0.5

    def chunk_attend(args):
        c, qc = args
        t = c * MOBA_Q_CHUNK + jnp.arange(MOBA_Q_CHUNK)
        own = (c * MOBA_Q_CHUNK) // MOBA_BLOCK
        gate = jnp.einsum('bhqd,bhnd->bhqn', qc, k_mean).astype(jnp.float32)
        gate = jnp.where(jnp.arange(nb) < own, gate, -jnp.inf)
        _, sel = lax.top_k(gate, ksel)
        valid = sel < own
        k_s = gather(k_blocks, sel)
        v_s = gather(v_blocks, sel)
        s_sel = jnp.einsum('bhqd,bhqnkd->bhqnk', qc, k_s).astype(jnp.float32) * scale
        s_sel = jnp.where(valid[..., None], s_sel, -jnp.inf).reshape(B, N_HEADS, MOBA_Q_CHUNK, ksel * MOBA_BLOCK)
        k_o = lax.dynamic_slice_in_dim(k_pad, own * MOBA_BLOCK, MOBA_BLOCK, axis=2)
        v_o = lax.dynamic_slice_in_dim(v_pad, own * MOBA_BLOCK, MOBA_BLOCK, axis=2)
        s_own = jnp.einsum('bhqd,bhkd->bhqk', qc, k_o).astype(jnp.float32) * scale
        causal = (own * MOBA_BLOCK + jnp.arange(MOBA_BLOCK))[None, :] <= t[:, None]
        s_own = jnp.where(causal, s_own, -jnp.inf)
        p = jax.nn.softmax(jnp.concatenate([s_sel, s_own], axis=-1), axis=-1).astype(qc.dtype)
        p_sel = p[..., :ksel * MOBA_BLOCK].reshape(B, N_HEADS, MOBA_Q_CHUNK, ksel, MOBA_BLOCK)
        p_own = p[..., ksel * MOBA_BLOCK:]
        return (jnp.einsum('bhqnk,bhqnkd->bhqd', p_sel, v_s)
                + jnp.einsum('bhqk,bhkd->bhqd', p_own, v_o))

    out = lax.map(chunk_attend, (jnp.arange(n_chunks), q_chunks))
    out = out.transpose(1, 0, 3, 2, 4).reshape(B, S, ATTN_DIM)
    return out @ w_o

def second_inputs(seed: int = 0) -> dict:
    key = jax.random.key(seed)
    ks = jax.random.split(key, 18)
    f32 = jnp.float32

    def w(k, shape, fan_in):
        return jax.random.normal(k, shape, f32) * (fan_in ** -0.5)

    def gain(k, shape):
        return 1.0 + 0.02 * jax.random.normal(k, shape, f32)

    return {
        'x': jax.random.normal(ks[0], (BATCH, SEQ, D_MODEL), f32),
        'ffn1_norm': gain(ks[1], (DEPTH, D_MODEL)),
        'ffn1_w_gate': w(ks[2], (DEPTH, D_MODEL, D_FF), D_MODEL),
        'ffn1_w_up': w(ks[3], (DEPTH, D_MODEL, D_FF), D_MODEL),
        'ffn1_w_down': w(ks[4], (DEPTH, D_FF, D_MODEL), D_FF),
        'mix_norm': gain(ks[5], (DEPTH, D_MODEL)),
        'ffn2_norm': gain(ks[6], (DEPTH, D_MODEL)),
        'ffn2_w_gate': w(ks[7], (DEPTH, D_MODEL, D_FF), D_MODEL),
        'ffn2_w_up': w(ks[8], (DEPTH, D_MODEL, D_FF), D_MODEL),
        'ffn2_w_down': w(ks[9], (DEPTH, D_FF, D_MODEL), D_FF),
        'a_w_qkv': w(ks[10], (N_A_LAYERS, D_MODEL, 3 * ATTN_DIM), D_MODEL),
        'a_w_o': w(ks[11], (N_A_LAYERS, ATTN_DIM, D_MODEL), ATTN_DIM),
        'kv_norm': gain(ks[12], (D_MODEL,)),
        'kv_w': w(ks[13], (D_MODEL, 2 * ATTN_DIM), D_MODEL),
        'b_w_q': w(ks[14], (N_B_LAYERS, D_MODEL, ATTN_DIM), D_MODEL),
        'b_w_o': w(ks[15], (N_B_LAYERS, ATTN_DIM, D_MODEL), ATTN_DIM),
        'final_norm': gain(ks[16], (D_MODEL,)),
    }

def second_block(x, ffn1_norm, ffn1_w_gate, ffn1_w_up, ffn1_w_down, mix_norm,
              ffn2_norm, ffn2_w_gate, ffn2_w_up, ffn2_w_down, a_w_qkv, a_w_o,
              kv_norm, kv_w, b_w_q, b_w_o, final_norm):
    pos = jnp.arange(x.shape[1], dtype=jnp.int32)
    h = x
    shared = None
    for layer in range(DEPTH):
        h = h + FFN_RESIDUAL_WEIGHT * swiglu(rmsnorm(h, ffn1_norm[layer]),
                                             ffn1_w_gate[layer], ffn1_w_up[layer], ffn1_w_down[layer])
        hn = rmsnorm(h, mix_norm[layer])
        if layer < N_A_LAYERS:
            h = h + mixer_a(hn, a_w_qkv[layer], a_w_o[layer], pos)
        else:
            j = layer - N_A_LAYERS
            h = h + mixer_b(hn, b_w_q[j], b_w_o[j], shared[0], shared[1], shared[2], pos)
        h = h + FFN_RESIDUAL_WEIGHT * swiglu(rmsnorm(h, ffn2_norm[layer]),
                                             ffn2_w_gate[layer], ffn2_w_up[layer], ffn2_w_down[layer])
        if layer == N_A_LAYERS - 1:
            shared = shared_kv(h, kv_norm, kv_w, pos)
    return rmsnorm(h, final_norm)


def setup_inputs(seed=0):
    out = dict(first_inputs(seed))
    for name, value in second_inputs(seed + 1).items():
        if name != "x":
            out[name + "_2"] = value
    return out


def reference(
    x, p, positions, norm_mix_pre, w_in, mla_q_norm, w_uq, mla_kv_norm, w_ukv, gqa_sink,
    w_branch_a, w_branch_b, w_branch_c, w_out, norm_mix_post, norm_ffn_pre, w_ffn_gate,
    w_ffn_up, w_ffn_down, norm_ffn_post, w_ple_proj, w_ple_gate, norm_ple, ffn1_norm_2,
    ffn1_w_gate_2, ffn1_w_up_2, ffn1_w_down_2, mix_norm_2, ffn2_norm_2, ffn2_w_gate_2,
    ffn2_w_up_2, ffn2_w_down_2, a_w_qkv_2, a_w_o_2, kv_norm_2, kv_w_2, b_w_q_2, b_w_o_2,
    final_norm_2,
):
    x = first_block(
        x, p, positions, norm_mix_pre, w_in, mla_q_norm, w_uq, mla_kv_norm, w_ukv, gqa_sink,
        w_branch_a, w_branch_b, w_branch_c, w_out, norm_mix_post, norm_ffn_pre, w_ffn_gate,
        w_ffn_up, w_ffn_down, norm_ffn_post, w_ple_proj, w_ple_gate, norm_ple,
    )
    return second_block(
        x, ffn1_norm_2, ffn1_w_gate_2, ffn1_w_up_2, ffn1_w_down_2, mix_norm_2, ffn2_norm_2,
        ffn2_w_gate_2, ffn2_w_up_2, ffn2_w_down_2, a_w_qkv_2, a_w_o_2, kv_norm_2, kv_w_2,
        b_w_q_2, b_w_o_2, final_norm_2,
    )


_drawn_inputs = setup_inputs


def setup_inputs(seed=0):
    import zlib

    import numpy as np

    out = dict(_drawn_inputs(seed))
    spreads = {}
    factors = {'mla_q_norm': 3.635,
     'gqa_sink': 5.743,
     'ffn1_norm_2': 8.0,
     'mix_norm_2': 8.0,
     'ffn2_norm_2': 8.0,
     'kv_norm_2': 8.0,
     'final_norm_2': 2.727}
    for name, (base, spread) in spreads.items():
        noise = np.random.default_rng([zlib.crc32(name.encode()), seed]).standard_normal(out[name].shape)
        drawn = base * np.exp(spread * noise) if base else spread * noise
        out[name] = __import__('jax').numpy.asarray(drawn.astype(out[name].dtype))
    for name, factor in factors.items():
        out[name] = (out[name] * factor).astype(out[name].dtype)
    return out
```

```python
import math
from contextlib import ExitStack

import numpy as np

import concourse.bass as bass
from concourse import mybir

P = 128
S = 256
T = S // P
D = 1024
DT = D // P
DEPTH = 2
PLE = 256
EPS = 1e-6

H1 = 8
NOPE, ROPE, VD = 64, 32, 64
QK = NOPE + ROPE
Q_LORA, KV_LORA = 384, 128
LORA = Q_LORA + KV_LORA
G_HD, G_KV = 64, 2
THETA1 = 10000.0
FGROUPS = 4
FW = D // FGROUPS
Z_SMALL = LORA + ROPE + H1 * G_HD + 2 * G_KV * G_HD
Z_QC = LORA + ROPE
Z_KC = Z_QC + H1 * G_HD
Z_VC = Z_KC + G_KV * G_HD
Z_CUTS = (0, 512, 1024, Z_SMALL)
FFN = 2816
CH = 256
NCH = FFN // CH
H2, HD2, ROT = 16, 64, 16
THETA2 = 500000.0
WINDOWS = ((128, 1), (512, 4), (2048, 16))

SLOTS = 3
UW = 2048
BIG = 1e30
ANGLE_STEPS, SETUP_STEPS = 19, 33

F32 = mybir.dt.float32
F32R = mybir.dt.float32r
I32 = mybir.dt.int32
ALU = mybir.AluOpType
ACT = mybir.ActivationFunctionType
AX = mybir.AxisListType

U_Z, U_UQ, U_UKV, U_DFT = 0, 6, 8, 9
U_GATE_B, U_BR_B, U_GATE_A, U_BR_A, U_GATE_C, U_BR_C = 10, 14, 18, 22, 24, 28
U_OUT, U_PROJ, U_FFN, U_PGATE, UNITS1 = 30, 34, 35, 68, 72
UNITS_FFN = 3 * NCH

SPIN = "va"


def runs(*parts):
    return "".join(k * n for k, n in parts)


HALF1 = runs(("v", 6), ("a", 4), ("a", 2), ("v", 12), ("a", 2), ("v", 2), ("a", 2), ("v", 2),
             ("a", 2), ("v", 2), ("v", 2), ("a", 2), ("v", 2), ("a", 2))
HF_Z, HF_UQ, HF_UKV, HF_F, HF_GB, HF_BB, HF_GA, HF_BA, HF_GC, HF_BC, HF_OUT, HF_PROJ, HF_DOWN, HF_PG = (
    0, 6, 10, 12, 24, 26, 28, 30, 32, 34, 36, 38, 40, 42)
HALF2 = runs(("v", 2), ("a", 6), ("v", 2), ("v", 2), ("a", 4), ("v", 2), ("a", 2), ("v", 2), ("v", 2))
TURN1 = runs(("v", 4), ("v", 2), ("v", 2), ("a", 2), ("v", 2), ("a", 4), ("v", 4), ("a", 16),
             ("v", 4), ("v", 4), ("v", 2 * NCH), ("v", 4))
TN_MIX, TN_P, TN_C, TN_QC, TN_KC, TN_Q, TN_K, TN_HEAD, TN_MERGE, TN_FFN, TN_HID, TN_PLE = (
    0, 4, 6, 8, 10, 12, 16, 20, 36, 40, 44, 66)
TURN_FFN2 = ("v", 4 + 2 * NCH)
TURN2 = runs(TURN_FFN2, ("v", 4), ("a", 4), ("v", 4), ("a", 16), TURN_FFN2, ("v", 4), ("v", 4),
             TURN_FFN2, ("v", 4), ("a", 4), ("a", 16), TURN_FFN2)
SCORE1 = runs(("a", H1), ("v", H1))
SCORE2 = runs(("v", 2 * H2))
CLASSES = {
    "half": (HALF1, HALF2),
    "turn": (TURN1, TURN2),
    "score": (SCORE1, SCORE2),
    "gu": ("v" * (2 * NCH), "v" * (2 * NCH * 4)),
    "pair": ("v" * H1, "v" * H2),
}

BASE = 1
BY_DMA = ("landed", "gain_in", "aux_in")

PER_LAYER = dict(
    landed=32 * UNITS1 // SLOTS, hi=UNITS1, lo=UNITS1,
    half_done=len(HALF1), turn_done=len(TURN1), score_done=2 * H1, gu_done=2 * NCH, pair_done=H1,
    half_hi=3 * FGROUPS, turn_hi=TURN1.count("v") - 6, pair_hi=H1,
    squared=14, inverse=14, gain_in=48, aux_in=32, silu=2 * NCH,
    h_ready=6, c_ready=2, x_ready=6, e_ready=2, merged=2,
    q_ready=1, k_ready=1, kc_ready=1, shift=2 * H1, expd=H1, probs=2 * H1, alibi=H1,
    v_link=34, g_link=16,
)
for _c, (_one, _) in CLASSES.items():
    for _e in SPIN:
        PER_LAYER[f"{_c}_read_{_e}"] = _one.count(_e)
PER_CHUNK = dict(landed=32, hi=3, lo=3, used=2, gu_done=2, gu_read_v=2, turn_done=2, turn_hi=2,
                 turn_read_v=2, silu=2)


def unit_ends():
    used = 0

    def plain(n):
        nonlocal used
        out = [("used", used + i + 1) for i in range(n)]
        used += n
        return out

    def wide(units, hf):
        return [*plain(units - 1), ("half_done", hf + 2)]

    def ffn(gu, hf):
        out = [*plain(1), ("gu_done", gu + 2)]
        for c in range(1, NCH):
            out += [*plain(1), ("gu_done", gu + 2 * c + 2), *plain(1)]
        return [*out, ("half_done", hf + 2)]

    one = []
    for c in range(3):
        one += [*plain(1), ("half_done", HF_Z + 2 * c + 2)]
    one += [("half_done", HF_UQ + 2), ("half_done", HF_UQ + 4), ("half_done", HF_UKV + 2)]
    one += [("half_done", HF_F + 3 * FGROUPS)]
    for units, hf in ((4, HF_GB), (4, HF_BB), (4, HF_GA), (2, HF_BA), (4, HF_GC), (2, HF_BC),
                      (4, HF_OUT), (1, HF_PROJ)):
        one += wide(units, hf)
    one += ffn(0, HF_DOWN) + wide(4, HF_PG)
    assert len(one) == UNITS1
    per_layer, used = used, 0
    two = ffn(0, 0)
    for n in range(4):
        two += wide(4, 2 + 2 * n)
    two += ffn(2 * NCH, 10) + wide(4, 12) + wide(4, 14) + ffn(4 * NCH, 16)
    two += wide(4, 18) + wide(4, 20) + ffn(6 * NCH, 22)
    return one, two, per_layer


ENDS1, ENDS2, PER_LAYER["used"] = unit_ends()


class Place:

    def __init__(self):
        self.layer = None
        self.chunk = None

    def at(self, name, n):
        key = {"landed": "landed", "gain_in": "gain_in"}.get(name.rstrip("0123456789"), name)
        per = PER_LAYER[key]
        if self.layer is None:
            v = DEPTH * per + n
        elif n >= 0:
            v = self.layer * per + n
        else:
            assert DEPTH == 2
            v = self.layer * (per + n)
        if self.chunk is not None:
            v = v + self.chunk * PER_CHUNK[key]
        return v if key in BY_DMA else v + BASE

    def read(self, cls, k):
        one, two = CLASSES[cls]
        if self.layer is None and k >= 0:
            return two[k], f"{cls}_read_{two[k]}", two[: k + 1].count(two[k])
        if k >= 0:
            return one[k], f"{cls}_read_{one[k]}", one[: k + 1].count(one[k])
        e = one[len(one) + k]
        return e, f"{cls}_read_{e}", one[: len(one) + k + 1].count(e) - one.count(e)

    def end_of(self, u):
        if self.layer is None and u >= 0:
            return ENDS2[u]
        if u >= 0:
            return ENDS1[u]
        name, n = ENDS1[UNITS1 + u]
        return name, n - PER_LAYER[name]


def two_blocks(nc, A, out):
    ctx = ExitStack()
    with ctx:
        def sb(name, shape, dt=F32):
            return ctx.enter_context(nc.sbuf_tensor(name, shape, dt))

        def under(name, shape, dt=F32):
            with nc.sbuf_tensor(name, shape, dt) as t:
                return t

        raw = sb("raw", [P, SLOTS, UW])
        whi = sb("whi", [P, SLOTS, UW], F32R)
        wlo = sb("wlo", [P, SLOTS, UW], F32R)
        xs = sb("xs", [P, T, D])
        h = sb("h", [P, T * D])
        act_hi = sb("act_hi", [P, DT, S], F32R)
        act_lo = sb("act_lo", [P, DT, S], F32R)
        gains = sb("gains", [P, 2, D])
        hid = sb("hid", [P, T, CH])
        hid_hi = sb("hid_hi", [P, CH // P, S], F32R)
        hid_lo = sb("hid_lo", [P, CH // P, S], F32R)
        prob = sb("prob", [P, 2, T, S])
        probT = sb("probT", [P, 2, T, S])
        ident = sb("ident", [P, P])
        mask = sb("mask", [P, T, S])
        alibi = sb("alibi", [P, 2, T, S])
        stat = sb("stat", [P, 16, 2])
        soft = sb("soft", [P, 5, 4, 2])
        sink = sb("sink", [P, H1])
        half_pow = sb("half_pow", [P, 1])
        eps = sb("eps", [P, 1])
        slopes = sb("slopes", [P, H1])
        cs1 = sb("cs1", [P, 2, T, ROPE // 2])
        cs2 = sb("cs2", [P, 2, T, ROT // 2])
        posk = sb("posk", [P, S], I32)
        posq = sb("posq", [P, T], I32)
        posi = sb("posi", [P, 2, T], I32)
        posf = sb("posf", [P, 3, T])
        freq = sb("freq", [P, ROPE // 2])

        block1 = ExitStack()
        with block1:
            def b1(name, shape, dt=F32):
                return block1.enter_context(nc.sbuf_tensor(name, shape, dt))

            kfull = under("kfull", [P, T, H1, QK])
            four_hi = b1("four_hi", [P, DT, S], F32R)
            four_lo = b1("four_lo", [P, DT, S], F32R)
            co_hi = b1("co_hi", [P, LORA // P, S], F32R)
            co_lo = b1("co_lo", [P, LORA // P, S], F32R)
            zs = under("zs", [P, T, Z_SMALL])
            oc_hi = b1("oc_hi", [P, H1 // 2, S], F32R)
            oc_lo = b1("oc_lo", [P, H1 // 2, S], F32R)
            b1("under_zs", [P, T * Z_SMALL - H1 * S])
            gate = under("gate", [P, T, D])
            fa_hi = b1("fa_hi", [P, T, 2 * FW], F32R)
            fa_lo = b1("fa_lo", [P, T, 2 * FW], F32R)
            v1 = b1("v1", [P, T, H1, VD])
            qT = b1("qT", [P, H1, S])
            kT = b1("kT", [P, H1, S])
            qcT = b1("qcT", [P, H1 // 2, S])
            kcT = b1("kcT", [P, 2, S])
            kswap = b1("kswap", [P, T, G_KV * G_HD])
            vc = b1("vc", [P, T, G_KV * G_HD])
        block2 = ExitStack()
        with block2:
            def b2(name, shape, dt=F32):
                return block2.enter_context(nc.sbuf_tensor(name, shape, dt))

            q2 = b2("q2", [P, T, D])
            k2 = b2("k2", [P, T, D])
            v2 = b2("v2", [P, T, D])
            qT2 = b2("qT2", [P, H2 // 2, S])
            kT2 = b2("kT2", [P, H2 // 2, S])
            o2_hi = b2("o2_hi", [P, DT, S], F32R)
            o2_lo = b2("o2_lo", [P, DT, S], F32R)

        ps = ctx.enter_context(nc.psum_tensor("ps", [P, 8, 512], F32))
        hq = h[:, 0:T * H1 * QK].rearrange("p (t h c) -> p t h c", t=T, h=H1)
        ht = h[:, :].rearrange("p (t n) -> p t n", t=T)
        junk = prob[:, :, :, :].rearrange("p a t n -> p (a t n)")

        sems = {}

        def sem(name):
            if name not in sems:
                sems[name] = ctx.enter_context(nc.semaphore(name))
            return sems[name]

        counted = [sem(name) for name in PER_LAYER if name not in BY_DMA]
        landed = [sem(f"landed{s}") for s in range(SLOTS)]
        s_in = {n: sem(f"in_{n}") for n in ("x", "pos", "const", "mask", "out")}
        s_setup = sem("setup")
        s_setup_g = sem("setup_g")
        s_ident = sem("ident_ready")
        s_trig = sem("trig")
        blk = ctx.enter_context(nc.Block())

        def u_view(buf, u, kts, cols):
            return buf[:, u % SLOTS, 0:kts * cols].rearrange("p (k n) -> p k n", k=kts)

        def unit_words(u):
            if u < U_UQ:
                c = u // 2
                return 4 * (Z_CUTS[c + 1] - Z_CUTS[c])
            if u < U_UKV:
                return 3 * (H1 * QK // 2)
            return {U_UKV: 1024, U_DFT: 2 * 3 * S}.get(u, UW)

        @blk.sync
        def _(sp):
            w = Place()

            def load(u, parts):
                sp.wait_ge(sem("lo"), w.at("lo", u - SLOTS + 1))
                assert len(parts) == 2
                for dst, src in parts:
                    sp.dma_start(dst, src).then_inc(landed[u % SLOTS], 16)

            def block(name, li, k0, kts, n0, cols):
                src = A[name][bass.ds(li, 1), k0 * P:(k0 + kts) * P, n0:n0 + cols]
                return src.rearrange("a (k p) n -> p (a k) n", p=P)

            def wide(u, name, li, k0, n0=0):
                v = u_view(raw, u, 2, D)
                load(u, [(v[:, k:k + 1, :], block(name, li, k0 + k, 1, n0, D)) for k in range(2)])

            def ffn_units(u, names, li):
                wg, wu, wd = names

                def gu(u, k0, n0):
                    v = raw[:, u % SLOTS, :].rearrange("p (k g n) -> p k g n", k=4, g=2)
                    parts = []
                    for g, name in enumerate((wg, wu)):
                        src = A[name][bass.ds(li, 1), k0 * P:(k0 + 4) * P, bass.ds(n0, CH)]
                        parts.append((v[:, :, g, :], src.rearrange("a (k p) n -> p (a k) n", p=P)))
                    load(u, parts)

                def down(u, row0):
                    v = u_view(raw, u, 2, D)
                    parts = []
                    for k in range(2):
                        src = A[wd][bass.ds(li, 1), bass.ds(row0 + k * P, P), :]
                        parts.append((v[:, k, :], src.rearrange("a p n -> p (a n)")))
                    load(u, parts)

                gu(u, 0, 0)
                gu(u + 1, 4, 0)
                gu(u + 2, 0, CH)
                gu(u + 3, 4, CH)
                down(u + 4, 0)
                with sp.Fori(0, NCH - 3) as i:
                    w.chunk = i
                    gu(u + 5, 0, i * CH + 2 * CH)
                    gu(u + 6, 4, i * CH + 2 * CH)
                    down(u + 7, i * CH + CH)
                w.chunk = None
                last = u + UNITS_FFN - 4
                gu(last, 0, (NCH - 1) * CH)
                gu(last + 1, 4, (NCH - 1) * CH)
                down(last + 2, (NCH - 2) * CH)
                down(last + 3, (NCH - 1) * CH)

            sp.dma_start(xs[:, :, :], A["x"][0, :, :].rearrange("(t p) n -> p t n", p=P)).then_inc(s_in["x"], 16)
            sp.dma_start(posk[:, :], A["positions"][0:1, :].partition_broadcast(P).rearrange("p a n -> p (a n)")).then_inc(s_in["pos"], 16)
            for t in range(T):
                sp.dma_start(posq[:, t:t + 1], A["positions"][0, t * P:(t + 1) * P].rearrange("(p a) -> p a", a=1))\
                    .then_inc(s_in["pos"], 16)
            sp.dma_start(freq[:, :], A["freq1"][0:1, :].partition_broadcast(P).rearrange("p a n -> p (a n)")).then_inc(s_in["pos"], 16)
            sp.dma_start(cs2[:, :, :, :], A["trig2"][:, :, :].rearrange("c (t p) n -> p c t n", p=P)).then_inc(s_in["const"], 16)
            with sp.Fori(0, DEPTH) as li:
                w.layer = li
                for c in range(3):
                    n0, cols = Z_CUTS[c], Z_CUTS[c + 1] - Z_CUTS[c]
                    for j in range(2):
                        v = u_view(raw, 2 * c + j, 4, cols)
                        load(2 * c + j, [(v[:, k:k + 2, :], block("w_in", li, 4 * j + k, 2, n0, cols)) for k in (0, 2)])
                for j in range(2):
                    cols = H1 * QK // 2
                    v = u_view(raw, U_UQ + j, 3, cols)
                    load(U_UQ + j, [(v[:, 0:2, :], block("w_uq", li, 0, 2, j * cols, cols)),
                                    (v[:, 2:3, :], block("w_uq", li, 2, 1, j * cols, cols))])
                v = u_view(raw, U_UKV, 1, D)
                load(U_UKV, [(v[:, :, n:n + 512], block("w_ukv", li, 0, 1, n, 512)) for n in (0, 512)])
                v = u_view(raw, U_DFT, 2, 3 * S)
                load(U_DFT, [(v[:, k, :], A["dft"][k * P:(k + 1) * P, :]) for k in range(2)])
                for u0, g0, br, name, tiles in ((U_GATE_B, 1, U_BR_B, "w_branch_b", 8),
                                                (U_GATE_A, 0, U_BR_A, "w_branch_a", 4),
                                                (U_GATE_C, 2, U_BR_C, "w_branch_c", 4)):
                    for j in range(4):
                        wide(u0 + j, "w_in", li, 2 * j, Z_SMALL + g0 * D)
                    for j in range(tiles // 2):
                        wide(br + j, name, li, 2 * j)
                for j in range(4):
                    wide(U_OUT + j, "w_out", li, 2 * j)
                wide(U_PROJ, "w_ple_proj", li, 0)
                ffn_units(U_FFN, ("w_ffn_gate", "w_ffn_up", "w_ffn_down"), li)
                for j in range(4):
                    wide(U_PGATE + j, "w_ple_gate", li, 2 * j)
            w.layer = None
            u = 0
            ffn1 = ("ffn1_w_gate_2", "ffn1_w_up_2", "ffn1_w_down_2")
            ffn2 = ("ffn2_w_gate_2", "ffn2_w_up_2", "ffn2_w_down_2")
            ffn_units(u, ffn1, 0)
            u += UNITS_FFN
            for n in range(3):
                for j in range(4):
                    wide(u + j, "a_w_qkv_2", 0, 2 * j, n * D)
                u += 4
            for j in range(4):
                wide(u + j, "a_w_o_2", 0, 2 * j)
            u += 4
            ffn_units(u, ffn2, 0)
            u += UNITS_FFN
            for n in range(2):
                for j in range(4):
                    v = u_view(raw, u + j, 2, D)
                    load(u + j, [(v[:, k, :], A["kv_w_2"][(2 * j + k) * P:(2 * j + k + 1) * P, n * D:(n + 1) * D])
                                 for k in range(2)])
                u += 4
            ffn_units(u, ffn1, 1)
            u += UNITS_FFN
            for name in ("b_w_q_2", "b_w_o_2"):
                for j in range(4):
                    wide(u + j, name, 0, 2 * j)
                u += 4
            ffn_units(u, ffn2, 1)
            for t in range(T):
                sp.wait_ge(sem("result"), t + 1)
                sp.dma_start(out[0, t * P:(t + 1) * P, :], ht[:, t, :]).then_inc(s_in["out"], 16)
            sp.wait_ge(s_in["out"], 16 * T)

        @blk.tensor
        def _(pe):
            w = Place()

            def free_before(cls, k):
                _, name, n = w.read(cls, k - 2)
                pe.wait_ge(sem(name), w.at(name, n))

            def was_read(cls, k):
                _, name, n = w.read(cls, k)
                pe.wait_ge(sem(name), w.at(name, n))

            def unit_there(u):
                pe.wait_ge(sem("lo"), w.at("lo", u + 1))

            def product(outs, hi, lo, whs, wls, start, stop):
                for o, a in zip(outs, whs):
                    nc.tensor.matmul(o, hi, a, start=start, stop=False)
                for o, a in zip(outs, wls):
                    nc.tensor.matmul(o, hi, a, start=False, stop=False)
                for o, a in zip(outs, whs):
                    last = nc.tensor.matmul(o, lo, a, start=False, stop=stop)
                return last

            def turn(k, src, n, rows=P, dst=None):
                free_before("turn", k)
                bank = ps[:, 2 + k % 2, :]
                for j in range(n):
                    last = nc.tensor.transpose(bank[0:rows, j * P:(j + 1) * P], src(j), ident[:, :])
                last.then_inc(sem("turn_done"), 1)

            def turn_rows(k, ready, src=None):
                src = ht if src is None else src
                for t in range(T):
                    ready(t)
                    for g in range(2):
                        turn(k + 2 * t + g, lambda j: src[:, t, (4 * g + j) * P:(4 * g + j + 1) * P], 4)

            def wide_job(u, units, hf, hi, lo, ready=None, k0=0):
                for j in range(units):
                    unit_there(u + j)
                    vh, vl = u_view(whi, u + j, 2, D), u_view(wlo, u + j, 2, D)
                    for t in range(T):
                        if j == 0:
                            free_before("half", hf + t)
                        for k in range(2):
                            kt = 2 * j + k
                            if ready is not None:
                                ready(t, kt)
                            outs = [ps[:, 4 + 2 * t + n, :] for n in range(2)]
                            last = product(outs, hi[:, kt, t * P:(t + 1) * P], lo[:, kt, t * P:(t + 1) * P],
                                           [vh[:, k, n * 512:(n + 1) * 512] for n in range(2)],
                                           [vl[:, k, n * 512:(n + 1) * 512] for n in range(2)],
                                           j == 0 and k == 0, j == units - 1 and k == 1)
                        if j == units - 1:
                            last.then_inc(sem("half_done"), 1)
                    if j < units - 1:
                        last.then_inc(sem("used"), 1)

            def rows_ready(k):
                def ready(t, kt):
                    if kt % 4 == 0:
                        was_read("turn", k + 2 * t + kt // 4)
                return ready

            def ffn(u, gu, tn, hf, rows):
                def gate_up(u, gu, ready=None):
                    def tile(t):
                        free_before("gu", gu + t)
                        for j in range(2):
                            if t == 0:
                                unit_there(u + j)
                            vh, vl = u_view(whi, u + j, 4, 512), u_view(wlo, u + j, 4, 512)
                            for k in range(4):
                                kt = 4 * j + k
                                if ready is not None:
                                    ready(t, kt)
                                last = product([ps[:, t, :]], act_hi[:, kt, t * P:(t + 1) * P],
                                               act_lo[:, kt, t * P:(t + 1) * P],
                                               [vh[:, k, :]], [vl[:, k, :]], kt == 0, kt == DT - 1)
                            if t == T - 1 and j == 0:
                                last.then_inc(sem("used"), 1)
                        last.then_inc(sem("gu_done"), 1)
                    return tile

                def turn_hidden(n, tn):
                    for t in range(T):
                        pe.wait_ge(sem("gu_read_v"), w.at("gu_read_v", n + t + 1))
                        turn(tn + t, lambda j: hid[:, t, j * P:(j + 1) * P], CH // P)

                def down(u, tn, start=False, stop=False):
                    unit_there(u)
                    vh, vl = u_view(whi, u, 2, D), u_view(wlo, u, 2, D)
                    for t in range(T):
                        if start:
                            free_before("half", hf + t)
                        was_read("turn", tn + t)
                        for k in range(2):
                            outs = [ps[:, 4 + 2 * t + n, :] for n in range(2)]
                            last = product(outs, hid_hi[:, k, t * P:(t + 1) * P], hid_lo[:, k, t * P:(t + 1) * P],
                                           [vh[:, k, n * 512:(n + 1) * 512] for n in range(2)],
                                           [vl[:, k, n * 512:(n + 1) * 512] for n in range(2)],
                                           start and k == 0, stop and k == 1)
                        if stop:
                            last.then_inc(sem("half_done"), 1)
                    if not stop:
                        last.then_inc(sem("used"), 1)

                def chunk(u, gu, tn, start):
                    tile = gate_up(u, gu)
                    tile(0)
                    turn_hidden(gu - T, tn)
                    tile(1)
                    down(u + 2, tn, start=start)

                tile = gate_up(u, gu, rows)
                tile(0)
                tile(1)
                chunk(u + 2, gu + 2, tn, True)
                with pe.Fori(0, NCH - 3) as i:
                    w.chunk = i
                    chunk(u + 5, gu + 4, tn + 2, False)
                w.chunk = None
                last = NCH - 1
                chunk(u + UNITS_FFN - 4, gu + 2 * last, tn + 2 * (last - 1), False)
                turn_hidden(gu + 2 * last, tn + 2 * last)
                down(u + UNITS_FFN - 1, tn + 2 * last, stop=True)

            def head(i, sc, tn, q, k, v, causal):
                rows = q[0].shape[0]

                def score():
                    free_before("score", sc)
                    for t in range(T):
                        cols = (t + 1) * P if causal else S
                        last = nc.tensor.matmul(ps[:, sc % 2, t * S:t * S + cols], q[t], k[:, 0:cols],
                                                start=True, stop=True)
                    last.then_inc(sem("score_done"), 1)

                def turn_probs():
                    free_before("turn", tn)
                    pe.wait_ge(sem("probs"), w.at("probs", sc + 1))
                    for kt in range(T):
                        for t in range(kt if causal else 0, T):
                            last = nc.tensor.transpose(ps[:, 2 + tn % 2, kt * S + t * P:kt * S + (t + 1) * P],
                                                       prob[:, sc % 2, t, kt * P:(kt + 1) * P], ident[:, :])
                    last.then_inc(sem("turn_done"), 1)

                def output():
                    pair, odd = sc // 2, sc % 2
                    if not odd:
                        free_before("pair", pair)
                    was_read("turn", tn)
                    o = ps[VD * odd:VD * (odd + 1), 5 + 2 * (pair % 2), :]
                    for kt in range(T):
                        c0 = kt * P if causal else 0
                        last = nc.tensor.matmul(o[:, c0:S], v[:, kt], probT[:, sc % 2, kt, c0:S],
                                                start=kt == 0, stop=kt == T - 1)
                    if odd:
                        last.then_inc(sem("pair_done"), 1)

                return score, turn_probs, output

            def attend(heads, extra=None):
                n = len(heads)
                heads[0][0]()
                for s in range(n + 2):
                    if s + 1 < n:
                        heads[s + 1][0]()
                    if 0 <= s - 2:
                        heads[s - 2][2]()
                    if 0 <= s - 1 < n:
                        heads[s - 1][1]()
                    if extra and s in extra:
                        extra[s]()

            def halves2(pT):
                return [pT[:, t * P:(t + 1) * P] for t in range(T)]

            def layer1():
                turn_rows(TN_MIX, lambda t: pe.wait_ge(sem("h_ready"), w.at("h_ready", t + 1)))
                pe.wait_ge(sem("aux_in"), w.at("aux_in", 32))
                for t in range(T):
                    turn(TN_P + t, lambda j: probT[:, 0, t, j * P:(j + 1) * P], PLE // P)
                ready = rows_ready(TN_MIX)
                for c in range(3):
                    cols = Z_CUTS[c + 1] - Z_CUTS[c]
                    for t in range(T):
                        free_before("half", HF_Z + 2 * c + t)
                        for j in range(2):
                            u = U_Z + 2 * c + j
                            if t == 0:
                                unit_there(u)
                            vh, vl = u_view(whi, u, 4, cols), u_view(wlo, u, 4, cols)
                            for k in range(4):
                                kt = 4 * j + k
                                if c == 0:
                                    ready(t, kt)
                                last = product([ps[:, 4 + 2 * t, 0:cols]], act_hi[:, kt, t * P:(t + 1) * P],
                                               act_lo[:, kt, t * P:(t + 1) * P],
                                               [vh[:, k, :]], [vl[:, k, :]], kt == 0, kt == DT - 1)
                            if t == T - 1 and j == 0:
                                last.then_inc(sem("used"), 1)
                        last.then_inc(sem("half_done"), 1)
                for t in range(T):
                    pe.wait_ge(sem("c_ready"), w.at("c_ready", t + 1))
                    turn(TN_C + t, lambda j: zs[:, t, j * P:(j + 1) * P], LORA // P)
                cols = H1 * QK // 2
                for j in range(2):
                    u = U_UQ + j
                    unit_there(u)
                    vh, vl = u_view(whi, u, 3, cols), u_view(wlo, u, 3, cols)
                    for t in range(T):
                        free_before("half", HF_UQ + 2 * j + t)
                        if j == 0:
                            was_read("turn", TN_C + t)
                        for k in range(3):
                            last = product([ps[:, 4 + 2 * t, 0:cols]], co_hi[:, k, t * P:(t + 1) * P],
                                           co_lo[:, k, t * P:(t + 1) * P], [vh[:, k, :]], [vl[:, k, :]],
                                           k == 0, k == 2)
                        last.then_inc(sem("half_done"), 1)
                unit_there(U_UKV)
                vh, vl = u_view(whi, U_UKV, 1, D), u_view(wlo, U_UKV, 1, D)
                for t in range(T):
                    free_before("half", HF_UKV + t)
                    last = product([ps[:, 4 + 2 * t + n, :] for n in range(2)],
                                   co_hi[:, 3, t * P:(t + 1) * P], co_lo[:, 3, t * P:(t + 1) * P],
                                   [vh[:, 0, n * 512:(n + 1) * 512] for n in range(2)],
                                   [vl[:, 0, n * 512:(n + 1) * 512] for n in range(2)], True, True)
                    last.then_inc(sem("half_done"), 1)

                dh, dl = u_view(whi, U_DFT, 2, 3 * S), u_view(wlo, U_DFT, 2, 3 * S)

                def over_width(g):
                    for t in range(T):
                        hf = HF_F + 3 * g + t
                        free_before("half", hf)
                        for k in range(2):
                            last = product([ps[:, 4 + 2 * (hf % 2), :]], act_hi[:, 2 * g + k, t * P:(t + 1) * P],
                                           act_lo[:, 2 * g + k, t * P:(t + 1) * P],
                                           [dh[:, k, 0:2 * S]], [dl[:, k, 0:2 * S]], k == 0, k == 1)
                        last.then_inc(sem("half_done"), 1)

                def over_tokens(g):
                    hf = HF_F + 3 * g + 2
                    free_before("half", hf)
                    for t in range(T):
                        was_read("half", HF_F + 3 * g + t)
                    for j in range(2):
                        for t in range(T):
                            for part, c0 in ((0, 0), (1, 2 * S)):
                                a = part * FW + j * P
                                last = product([ps[:, 4 + 2 * (hf % 2), j * S:(j + 1) * S]],
                                               fa_hi[:, t, a:a + P], fa_lo[:, t, a:a + P],
                                               [dh[:, t, c0:c0 + S]], [dl[:, t, c0:c0 + S]],
                                               t == 0 and part == 0, t == T - 1 and part == 1)
                    last.then_inc(sem("half_done"), 1)

                unit_there(U_DFT)
                over_width(0)
                was_read("half", HF_Z + 5)
                for t in range(T):
                    turn(TN_QC + t, lambda j: zs[:, t, Z_QC + j * P:Z_QC + (j + 1) * P], H1 // 2)
                pe.wait_ge(sem("kc_ready"), w.at("kc_ready", 1))
                for t in range(T):
                    turn(TN_KC + t, lambda j: (zs[:, t, Z_KC:Z_KC + P], kswap[:, t, :])[j], 2)
                pe.wait_ge(sem("q_ready"), w.at("q_ready", 1))
                for t in range(T):
                    for g in range(2):
                        turn(TN_Q + 2 * t + g, lambda j: hq[:, t, 4 * g + j, :], 4, QK)
                pe.wait_ge(sem("k_ready"), w.at("k_ready", 1))
                was_read("half", HF_UKV + 1)
                for t in range(T):
                    for g in range(2):
                        turn(TN_K + 2 * t + g, lambda j: kfull[:, t, 4 * g + j, :], 4, QK)
                for k in (TN_QC + 1, TN_KC + 1, TN_Q + 3, TN_K + 3):
                    was_read("turn", k)
                heads = []
                for i in range(H1):
                    heads.append(head(i, i, TN_HEAD + i, halves2(qT[0:QK, i, :]), kT[0:QK, i, :],
                                      v1[:, :, i, :], False))
                for i in range(H1):
                    n, odd = i // (H1 // G_KV), i % 2
                    part = slice(G_HD * odd, G_HD * (odd + 1))
                    heads.append(head(i, H1 + i, TN_HEAD + H1 + i, halves2(qcT[part, i // 2, :]),
                                      kcT[part, 0 if n == odd else 1, :],
                                      vc[:, :, n * G_HD:(n + 1) * G_HD], False))
                extra = {0: lambda: over_tokens(0)}
                for g in range(1, FGROUPS):
                    extra[4 * g - 2] = lambda g=g: over_width(g)
                    extra[4 * g] = lambda g=g: over_tokens(g)
                attend(heads, extra)
                was_read("pair", H1 - 2)
                was_read("pair", H1 - 1)
                wide_job(U_GATE_B, 4, HF_GB, act_hi, act_lo)
                was_read("half", HF_F + 3 * FGROUPS - 1)
                wide_job(U_BR_B, 4, HF_BB, four_hi, four_lo)
                wide_job(U_GATE_A, 4, HF_GA, act_hi, act_lo)
                wide_job(U_BR_A, 2, HF_BA, co_hi, co_lo)
                wide_job(U_GATE_C, 4, HF_GC, act_hi, act_lo)
                wide_job(U_BR_C, 2, HF_BC, oc_hi, oc_lo)
                turn_rows(TN_MERGE, lambda t: pe.wait_ge(sem("h_ready"), w.at("h_ready", 2 + t + 1)))
                wide_job(U_OUT, 4, HF_OUT, act_hi, act_lo, rows_ready(TN_MERGE))
                wide_job(U_PROJ, 1, HF_PROJ, hid_hi, hid_lo)
                turn_rows(TN_FFN, lambda t: pe.wait_ge(sem("h_ready"), w.at("h_ready", 4 + t + 1)))
                ffn(U_FFN, 0, TN_HID, HF_DOWN, rows_ready(TN_FFN))
                turn_rows(TN_PLE, lambda t: pe.wait_ge(sem("x_ready"), w.at("x_ready", 2 + t + 1)), xs)
                wide_job(U_PGATE, 4, HF_PG, act_hi, act_lo, rows_ready(TN_PLE))

            for s in counted:
                pe.sem_inc(s, BASE)
            pe.wait_ge(s_ident, 2)
            with pe.Fori(0, DEPTH) as li:
                w.layer = li
                layer1()
            w.layer = None

            u, gu, tn, hf, hr = 0, 0, 0, 0, 0

            def h_rows():
                nonlocal tn, hr
                base = hr
                turn_rows(tn, lambda t: pe.wait_ge(sem("h_ready"), w.at("h_ready", base + t + 1)))
                hr += 2
                tn += 4
                return rows_ready(tn - 4)

            def ffn_here():
                nonlocal u, gu, tn, hf
                rows = h_rows()
                ffn(u, gu, tn, hf, rows)
                u, gu, tn, hf = u + UNITS_FFN, gu + 2 * NCH, tn + 2 * NCH, hf + 2

            def wide_here(hi, lo, ready=None):
                nonlocal u, hf
                wide_job(u, 4, hf, hi, lo, ready)
                u, hf = u + 4, hf + 2

            def turn_heads(name, n, src):
                nonlocal tn
                pe.wait_ge(sem(name), w.at(name, n))
                for t in range(T):
                    for g in range(2):
                        turn(tn + 2 * t + g, lambda j: src[:, t, (4 * g + j) * P:(4 * g + j + 1) * P], 4)
                tn += 4

            def attend_here(sc, turned):
                nonlocal tn
                for k in turned:
                    was_read("turn", k)
                heads = []
                for i in range(H2):
                    part = slice(HD2 * (i % 2), HD2 * (i % 2 + 1))
                    heads.append(head(i, sc + i, tn + i, halves2(qT2[part, i // 2, :]), kT2[part, i // 2, :],
                                      v2[:, :, i * HD2:(i + 1) * HD2], True))
                attend(heads)
                tn += H2
                was_read("pair", (sc + H2) // 2 - 2)
                was_read("pair", (sc + H2) // 2 - 1)

            ffn_here()
            rows = h_rows()
            wide_here(act_hi, act_lo, rows)
            wide_here(act_hi, act_lo)
            wide_here(act_hi, act_lo)
            turn_heads("q_ready", 1, q2)
            turn_heads("k_ready", 1, k2)
            was_read("half", hf - 1)
            attend_here(0, (tn - 5, tn - 1))
            wide_here(o2_hi, o2_lo)
            ffn_here()
            rows = h_rows()
            wide_here(act_hi, act_lo, rows)
            wide_here(act_hi, act_lo)
            turn_heads("k_ready", 2, k2)
            keys_turned, values_read = tn - 1, hf - 1
            ffn_here()
            rows = h_rows()
            wide_here(act_hi, act_lo, rows)
            turn_heads("q_ready", 2, q2)
            was_read("half", values_read)
            attend_here(H2, (keys_turned, tn - 1))
            wide_here(o2_hi, o2_lo)
            ffn_here()

        def soft_of(i):
            return [soft[:, n, i % 4, :] for n in range(5)]

        @blk.scalar
        def _(act):
            w = Place()
            done = [0]

            def split(n):
                for _ in range(n):
                    u = done[0]
                    if w.layer is None and u == len(ENDS2):
                        return
                    act.wait_ge(landed[u % SLOTS], w.at(f"landed{u % SLOTS}", 32 * (u // SLOTS + 1)))
                    if not at_start:
                        name, k = w.end_of(u - SLOTS)
                        act.wait_ge(sem(name), w.at(name, k))
                    words = unit_words(u) if w.layer is not None else UW
                    nc.scalar.activation(whi[:, u % SLOTS, 0:words], raw[:, u % SLOTS, 0:words], ACT.Copy)\
                        .then_inc(sem("hi"), 1)
                    done[0] += 1

            def turned_hi(k, dst, n=4):
                act.wait_ge(sem("turn_done"), w.at("turn_done", k + 1))
                nc.scalar.activation(dst, ps[:, 2 + k % 2, 0:n * P].rearrange("p (j c) -> p j c", j=n),
                                     ACT.Copy).then_inc(sem("turn_hi"), 1)

            def turned_copy(k, dst, n=4, rows=P):
                act.wait_ge(sem("turn_done"), w.at("turn_done", k + 1))
                nc.scalar.activation(dst, ps[0:rows, 2 + k % 2, 0:n * P].rearrange("p (j c) -> p j c", j=n),
                                     ACT.Copy).then_inc(sem("turn_read_a"), 1)

            def turned_rows_hi(k):
                for t in range(T):
                    for g in range(2):
                        turned_hi(k + 2 * t + g, act_hi[:, 4 * g:4 * g + 4, t * P:(t + 1) * P])

            def half_there(hf):
                act.wait_ge(sem("half_done"), w.at("half_done", hf + 1))

            def half_bank(hf, banks=1):
                return ps[:, 4 + 2 * (hf % 2):4 + 2 * (hf % 2) + banks, :].rearrange("p b n -> p (b n)")

            def square(n, src):
                words = src.shape[-1]
                act.wait_ge(sem("squared"), w.at("squared", n))
                nc.scalar.activation(junk[:, 0:words], src, ACT.Square, scale=float(words) ** -0.5,
                                     accum_out=stat[:, n, 0:1])\
                    .then_inc(sem("squared"), 1)

            def ffn(gu, tn, silu_n):
                def silu(gu, t, tn=None):
                    act.wait_ge(sem("gu_done"), w.at("gu_done", gu + t + 1))
                    if tn is not None:
                        act.wait_ge(sem("turn_done"), w.at("turn_done", tn + t + 1))
                    nc.scalar.activation(hid[:, t, :], ps[:, t, 0:CH], ACT.Silu).then_inc(sem("silu"), 1)

                def hidden_hi(tn):
                    for t in range(T):
                        turned_hi(tn + t, hid_hi[:, :, t * P:(t + 1) * P], CH // P)

                def chunk(gu, tn):
                    silu(gu, 0, tn)
                    hidden_hi(tn)
                    split(1)
                    silu(gu, 1, tn)
                    split(2)

                silu(gu, 0)
                split(1)
                silu(gu, 1)
                split(1)
                chunk(gu + 2, tn)
                with act.Fori(0, NCH - 3) as i:
                    w.chunk = i
                    chunk(gu + 4, tn + 2)
                w.chunk = None
                done[0] += 3 * (NCH - 4)
                last = NCH - 1
                chunk(gu + 2 * last, tn + 2 * (last - 1))
                hidden_hi(tn + 2 * last)

            def exps(i, scale=None, sink_h=None, causal=False):
                _, nm, sm, _, es = soft_of(i)
                act.wait_ge(sem("shift"), w.at("shift", i + 1))
                if sink_h is not None:
                    nc.scalar.activation(es, nm, ACT.Exp, bias=sink[:, sink_h:sink_h + 1])
                for t in range(T):
                    cols = (t + 1) * P if causal else S
                    src = prob[:, i % 2, t, 0:cols] if scale is None else ps[:, i % 2, t * S:t * S + cols]
                    last = nc.scalar.activation(prob[:, i % 2, t, 0:cols], src, ACT.Exp, bias=nm[:, t:t + 1],
                                                scale=1.0 if scale is None else scale,
                                                accum_out=sm[:, t:t + 1])
                last.then_inc(sem("expd" if scale is None else "score_read_a"), 1)

            def probs_turned(sc, tn, causal):
                act.wait_ge(sem("turn_done"), w.at("turn_done", tn + 1))
                bank = ps[:, 2 + tn % 2, :].rearrange("p (k n) -> p k n", k=T)
                if causal:
                    nc.scalar.activation(probT[:, sc % 2, 0, :], bank[:, 0, :], ACT.Copy)
                    nc.scalar.activation(probT[:, sc % 2, 1, P:S], bank[:, 1, P:S], ACT.Copy)\
                        .then_inc(sem("turn_read_a"), 1)
                else:
                    nc.scalar.activation(probT[:, sc % 2, :, :], bank, ACT.Copy).then_inc(sem("turn_read_a"), 1)

            def pair_hi(pair, dst):
                act.wait_ge(sem("pair_done"), w.at("pair_done", pair + 1))
                nc.scalar.activation(dst, ps[:, 5 + 2 * (pair % 2), 0:S], ACT.Copy).then_inc(sem("pair_hi"), 1)

            def layer1():
                for t in range(T):
                    act.wait_ge(sem("x_ready"), w.at("x_ready", t - 1))
                    square(t, xs[:, t, :])
                turned_rows_hi(TN_MIX)
                for t in range(T):
                    turned_hi(TN_P + t, hid_hi[:, :, t * P:(t + 1) * P], PLE // P)
                split(2)
                for t in range(T):
                    act.wait_ge(sem("half_read_v"), w.at("half_read_v", HF_Z + t + 1))
                    square(2 + 2 * t, zs[:, t, 0:Q_LORA])
                    square(3 + 2 * t, zs[:, t, Q_LORA:LORA])
                split(4)
                for t in range(T):
                    turned_hi(TN_C + t, co_hi[:, :, t * P:(t + 1) * P])
                cols = H1 * QK // 2
                for j in range(2):
                    for t in range(T):
                        half_there(HF_UQ + 2 * j + t)
                        nc.scalar.activation(h[:, t * 2 * cols + j * cols:t * 2 * cols + (j + 1) * cols],
                                             half_bank(HF_UQ + 2 * j + t)[:, 0:cols], ACT.Copy)\
                            .then_inc(sem("half_read_a"), 1)
                    split(1)
                for t in range(T):
                    half_there(HF_UKV + t)
                    kv = half_bank(HF_UKV + t, 2).rearrange("p (h c) -> p h c", h=H1)
                    nc.scalar.activation(kfull[:, t, :, 0:NOPE], kv[:, :, 0:NOPE], ACT.Copy)
                    nc.scalar.activation(v1[:, t, :, :], kv[:, :, NOPE:NOPE + VD], ACT.Copy)\
                        .then_inc(sem("half_read_a"), 1)
                split(1)

                def width_hi(g):
                    for t in range(T):
                        hf = HF_F + 3 * g + t
                        half_there(hf)
                        nc.scalar.activation(fa_hi[:, t, :], half_bank(hf), ACT.Copy).then_inc(sem("half_hi"), 1)

                def tokens_hi(g):
                    hf = HF_F + 3 * g + 2
                    half_there(hf)
                    nc.scalar.activation(four_hi[:, 2 * g:2 * g + 2, :],
                                         half_bank(hf).rearrange("p (j c) -> p j c", j=2), ACT.Copy)\
                        .then_inc(sem("half_hi"), 1)

                width_hi(0)
                for t in range(T):
                    turned_copy(TN_QC + t, qcT[:, :, t * P:(t + 1) * P])
                for t in range(T):
                    for g in range(2):
                        turned_copy(TN_Q + 2 * t + g, qT[0:QK, 4 * g:4 * g + 4, t * P:(t + 1) * P], 4, QK)
                heads = 2 * H1
                for s in range(heads + 2):
                    if s < H1:
                        exps(s, scale=float(QK) ** -0.5)
                    elif s < heads:
                        exps(s, sink_h=s - H1)
                    if s >= 2 and s % 2:
                        pair = (s - 2) // 2
                        pair_hi(pair, (co_hi if pair < H1 // 2 else oc_hi)[:, pair % (H1 // 2), :])
                    if 1 <= s <= heads:
                        probs_turned(s - 1, TN_HEAD + s - 1, False)
                    if s % 4 == 0 and s // 4 < FGROUPS:
                        tokens_hi(s // 4)
                    if s % 4 == 2 and s // 4 + 1 < FGROUPS:
                        width_hi(s // 4 + 1)
                split(1)
                for gate_hf, tiles, before in ((HF_GB, 8, None), (HF_GA, 4, ("half_read_v", 6 + 12 + 2)),
                                               (HF_GC, 4, ("merged", 2))):
                    split(3)
                    for t in range(T):
                        half_there(gate_hf + t)
                        if before:
                            act.wait_ge(sem(before[0]), w.at(before[0], before[1] - 1 + t))
                        nc.scalar.activation(gate[:, t, :], half_bank(gate_hf + t, 2), ACT.Sigmoid)\
                            .then_inc(sem("half_read_a"), 1)
                    split(1 + tiles // 2)
                turned_rows_hi(TN_MERGE)
                split(3)
                for t in range(T):
                    half_there(HF_OUT + t)
                    square(6 + t, half_bank(HF_OUT + t, 2))
                split(1)
                for t in range(T):
                    act.wait_ge(sem("x_ready"), w.at("x_ready", t + 1))
                    square(8 + t, xs[:, t, :])
                for t in range(T):
                    half_there(HF_PROJ + t)
                    nc.scalar.activation(gate[:, t, :], half_bank(HF_PROJ + t, 2), ACT.Copy)\
                        .then_inc(sem("half_read_a"), 1)
                split(1)
                turned_rows_hi(TN_FFN)
                ffn(0, TN_HID, 0)
                for t in range(T):
                    half_there(HF_DOWN + t)
                    square(10 + t, half_bank(HF_DOWN + t, 2))
                split(1)
                turned_rows_hi(TN_PLE)
                split(3)
                for t in range(T):
                    half_there(HF_PG + t)
                    nc.scalar.activation(ht[:, t, :], half_bank(HF_PG + t, 2), ACT.Sigmoid)\
                        .then_inc(sem("half_read_a"), 1)
                split(1)
                for t in range(T):
                    act.wait_ge(sem("e_ready"), w.at("e_ready", t + 1))
                    square(12 + t, ht[:, t, :])

            act.wait_ge(s_setup, ANGLE_STEPS)
            nc.scalar.activation(cs1[:, :, :, :], cs1[:, :, :, :], ACT.Sin).then_inc(s_trig, 1)
            act.wait_ge(s_in["x"], 16)
            at_start = True
            w.layer = 0
            split(SLOTS)
            at_start = False
            with act.Fori(0, DEPTH) as li:
                w.layer = li
                done[0] = SLOTS
                layer1()
                assert done[0] == UNITS1 + SLOTS, done
            w.layer = None
            done[0] = SLOTS

            sq, tn, hf, gu, hv = 0, 0, 0, 0, 0

            def norm_squares(ready=None):
                nonlocal sq
                for t in range(T):
                    if ready is not None:
                        act.wait_ge(sem("half_read_v"), w.at("half_read_v", ready + t + 1))
                    elif sq == 0:
                        act.wait_ge(sem("x_ready"), w.at("x_ready", t - 1))
                    square(sq + t, xs[:, t, :])
                sq += T

            def rows_here():
                nonlocal tn
                turned_rows_hi(tn)
                tn += 4

            def ffn_here():
                nonlocal tn, hf, gu, hv
                rows_here()
                ffn(gu, tn, 0)
                tn, hf, gu, hv = tn + 2 * NCH, hf + T, gu + 2 * NCH, hv + T
                split(1)
                norm_squares(hv - T)

            def copy_out(dst):
                nonlocal hf
                split(3)
                for t in range(T):
                    half_there(hf + t)
                    nc.scalar.activation(dst[:, t, :], half_bank(hf + t, 2), ACT.Copy)\
                        .then_inc(sem("half_read_a"), 1)
                split(1)
                hf += T

            def turn_queries():
                nonlocal tn
                for t in range(T):
                    for g in range(2):
                        turned_copy(tn + 2 * t + g, qT2[:, 4 * g:4 * g + 4, t * P:(t + 1) * P])
                tn += 4

            def attend(sc):
                nonlocal tn
                for s in range(H2 + 2):
                    if s < H2:
                        exps(sc + s, causal=True)
                    if s >= 2 and s % 2:
                        pair = (s - 2) // 2
                        pair_hi((sc // 2) + pair, o2_hi[:, pair, :])
                    if 1 <= s <= H2:
                        probs_turned(sc + s - 1, tn + s - 1, True)
                tn += H2

            norm_squares()
            ffn_here()
            rows_here()
            copy_out(q2)
            copy_out(k2)
            copy_out(v2)
            turn_queries()
            tn += 4
            attend(0)
            split(4)
            hf, hv = hf + T, hv + T
            norm_squares(hv - T)
            ffn_here()
            norm_squares(hv - T)
            rows_here()
            copy_out(k2)
            copy_out(v2)
            tn += 4
            ffn_here()
            rows_here()
            copy_out(q2)
            turn_queries()
            attend(H2)
            split(4)
            hf, hv = hf + T, hv + T
            norm_squares(hv - T)
            ffn_here()

        @blk.vector
        def _(dve):
            w = Place()
            done = [0]
            links = [0]

            def link(ins):
                ins.then_inc(sem("v_link"), 1)
                links[0] += 1
                dve.wait_ge(sem("v_link"), w.at("v_link", links[0]))

            def split(n):
                for _ in range(n):
                    u = done[0]
                    if w.layer is None and u == len(ENDS2):
                        return
                    dve.wait_ge(sem("hi"), w.at("hi", u + 1))
                    words = unit_words(u) if w.layer is not None else UW
                    nc.vector.tensor_tensor(wlo[:, u % SLOTS, 0:words], raw[:, u % SLOTS, 0:words],
                                            whi[:, u % SLOTS, 0:words].bitcast(F32), ALU.subtract)\
                        .then_inc(sem("lo"), 1)
                    done[0] += 1

            def rest(dst, src, hi):
                return nc.vector.tensor_tensor(dst, src, hi.bitcast(F32), ALU.subtract)

            hi_n = [0]

            def turned_lo(k, dst, hi, n=4):
                hi_n[0] += 1
                dve.wait_ge(sem("turn_hi"), w.at("turn_hi", hi_n[0]))
                rest(dst, ps[:, 2 + k % 2, 0:n * P].rearrange("p (j c) -> p j c", j=n), hi)\
                    .then_inc(sem("turn_read_v"), 1)

            def turned_copy(k, dst, n=4, rows=P):
                dve.wait_ge(sem("turn_done"), w.at("turn_done", k + 1))
                nc.vector.tensor_copy(dst, ps[0:rows, 2 + k % 2, 0:n * P].rearrange("p (j c) -> p j c", j=n))\
                    .then_inc(sem("turn_read_v"), 1)

            def turned_rows_lo(k, t=None):
                for tt in range(T) if t is None else (t,):
                    for g in range(2):
                        at = (slice(None), slice(4 * g, 4 * g + 4), slice(tt * P, (tt + 1) * P))
                        turned_lo(k + 2 * tt + g, act_lo[at], act_hi[at])

            def half_there(hf):
                dve.wait_ge(sem("half_done"), w.at("half_done", hf + 1))

            def half_bank(hf, banks=1):
                return ps[:, 4 + 2 * (hf % 2):4 + 2 * (hf % 2) + banks, :].rearrange("p b n -> p (b n)")

            def scaled(n, g, dst, src, cols=None):
                dve.wait_ge(sem("inverse"), w.at("inverse", n + 1))
                dve.wait_ge(sem(f"gain_in{g % 2}"), w.at(f"gain_in{g % 2}", 16 * (g // 2 + 1)))
                row = gains[:, g % 2, :] if cols is None else gains[:, g % 2, cols[0]:cols[1]]
                return nc.vector.scalar_tensor_tensor(dst, src, stat[:, n, 1:2], row, ALU.mult, ALU.mult)

            def norm_rows(n, g, k, ready="h_ready"):
                for t in range(T):
                    scaled(n + t, g, ht[:, t, :], xs[:, t, :]).then_inc(sem(ready), 1)
                if k is not None:
                    turned_rows_lo(k)

            def ffn(gu, tn):
                def times_up(gu, t):
                    dve.wait_ge(sem("silu"), w.at("silu", gu + t + 1))
                    nc.vector.tensor_tensor(hid[:, t, :], hid[:, t, :], ps[:, t, CH:2 * CH], ALU.mult)\
                        .then_inc(sem("gu_read_v"), 1)

                def hidden_lo(tn):
                    for t in range(T):
                        at = (slice(None), slice(None), slice(t * P, (t + 1) * P))
                        turned_lo(tn + t, hid_lo[at], hid_hi[at], CH // P)

                def chunk(gu, tn):
                    times_up(gu, 0)
                    hidden_lo(tn)
                    split(1)
                    times_up(gu, 1)
                    split(2)

                times_up(gu, 0)
                split(1)
                times_up(gu, 1)
                split(1)
                chunk(gu + 2, tn)
                with dve.Fori(0, NCH - 3) as i:
                    w.chunk = i
                    chunk(gu + 4, tn + 2)
                w.chunk = None
                done[0] += 3 * (NCH - 4)
                hi_n[0] += T * (NCH - 4)
                last = NCH - 1
                chunk(gu + 2 * last, tn + 2 * (last - 1))
                hidden_lo(tn + 2 * last)

            def shifts(i, add=None, scale=1.0, sink_h=None, causal=False):
                mx, nm, _, _, _ = soft_of(i)
                dve.wait_ge(sem("score_done"), w.at("score_done", i + 1))
                if add is None:
                    link(nc.vector.tensor_reduce(mx, ps[:, i % 2, :].rearrange("p (t n) -> p t n", t=T),
                                                 AX.X, ALU.max))
                    nc.vector.tensor_scalar(nm, mx, -scale, None, ALU.mult).then_inc(sem("shift"), 1)
                    return
                if i >= 2:
                    dve.wait_ge(sem("turn_done"), w.at("turn_done", turn_of(i - 2) + 1))
                nc.vector.memset(nm, 0.0)
                for t in range(T):
                    cols = (t + 1) * P if causal else S
                    last = nc.vector.tensor_tensor_reduce(
                        out=prob[:, i % 2, t, 0:cols], in0=ps[:, i % 2, t * S:t * S + cols],
                        in1=add[:, t, 0:cols], scale=scale, scalar=-3e38, op0=ALU.add, op1=ALU.max,
                        accum_out=mx[:, t:t + 1])
                last.then_inc(sem("score_read_v"), 1)
                _, name, n = w.read("score", i)
                dve.wait_ge(sem(name), w.at(name, n))
                if sink_h is None:
                    nc.vector.tensor_scalar(nm, mx, -1.0, None, ALU.mult).then_inc(sem("shift"), 1)
                else:
                    nc.vector.tensor_scalar(nm, mx, sink[:, sink_h:sink_h + 1], -1.0, ALU.max, ALU.mult)\
                        .then_inc(sem("shift"), 1)

            def normalise(i, ready, with_sink=False, causal=False):
                _, _, sm, rs, es = soft_of(i)
                dve.wait_ge(sem(ready[0]), w.at(*ready))
                if with_sink:
                    link(nc.vector.tensor_tensor(sm, sm, es, ALU.add))
                link(nc.vector.reciprocal(rs, sm))
                for t in range(T):
                    cols = (t + 1) * P if causal else S
                    last = nc.vector.tensor_scalar(prob[:, i % 2, t, 0:cols], prob[:, i % 2, t, 0:cols],
                                                   rs[:, t:t + 1], None, ALU.mult)
                last.then_inc(sem("probs"), 1)

            def pair_lo(pair, dst, hi):
                dve.wait_ge(sem("pair_hi"), w.at("pair_hi", pair + 1))
                rest(dst, ps[:, 5 + 2 * (pair % 2), 0:S], hi).then_inc(sem("pair_read_v"), 1)

            def residual(n, g, hf):
                for t in range(T):
                    scaled(n + t, g, ht[:, t, :], half_bank(hf + t, 2)).then_inc(sem("half_read_v"), 1)
                    _, name, k = w.read("half", hf + t)
                    dve.wait_ge(sem(name), w.at(name, k))
                    nc.vector.tensor_tensor(xs[:, t, :], xs[:, t, :], ht[:, t, :], ALU.add)\
                        .then_inc(sem("x_ready"), 1)

            def layer1():
                nonlocal half_hi
                half_hi = 0
                norm_rows(0, 0, TN_MIX)
                for t in range(T):
                    at = (slice(None), slice(None), slice(t * P, (t + 1) * P))
                    turned_lo(TN_P + t, hid_lo[at], hid_hi[at], PLE // P)

                def z_half(c, t):
                    hf = HF_Z + 2 * c + t
                    n0, cols = Z_CUTS[c], Z_CUTS[c + 1] - Z_CUTS[c]
                    half_there(hf)
                    nc.vector.tensor_copy(zs[:, t, n0:n0 + cols], half_bank(hf)[:, 0:cols])\
                        .then_inc(sem("half_read_v"), 1)

                z_half(0, 0)
                split(1)
                z_half(0, 1)
                split(1)
                z_half(1, 0)
                for t in range(T):
                    scaled(2 + 2 * t, 1, zs[:, t, 0:Q_LORA], zs[:, t, 0:Q_LORA], (0, Q_LORA))
                    scaled(3 + 2 * t, 1, zs[:, t, Q_LORA:LORA], zs[:, t, Q_LORA:LORA], (Q_LORA, LORA))\
                        .then_inc(sem("c_ready"), 1)
                split(1)
                z_half(1, 1)
                split(1)
                z_half(2, 0)
                split(1)
                z_half(2, 1)
                split(1)
                for t in range(T):
                    at = (slice(None), slice(None), slice(t * P, (t + 1) * P))
                    turned_lo(TN_C + t, co_lo[at], co_hi[at])
                split(3)

                def width_lo(g):
                    nonlocal half_hi
                    for t in range(T):
                        half_hi += 1
                        dve.wait_ge(sem("half_hi"), w.at("half_hi", half_hi))
                        rest(fa_lo[:, t, :], half_bank(HF_F + 3 * g + t), fa_hi[:, t, :])\
                            .then_inc(sem("half_read_v"), 1)

                def tokens_lo(g):
                    nonlocal half_hi
                    half_hi += 1
                    dve.wait_ge(sem("half_hi"), w.at("half_hi", half_hi))
                    rest(four_lo[:, 2 * g:2 * g + 2, :],
                         half_bank(HF_F + 3 * g + 2).rearrange("p (j c) -> p j c", j=2),
                         four_hi[:, 2 * g:2 * g + 2, :]).then_inc(sem("half_read_v"), 1)

                width_lo(0)
                for t in range(T):
                    turned_copy(TN_KC + t, kcT[:, :, t * P:(t + 1) * P], 2)
                for t in range(T):
                    for g in range(2):
                        turned_copy(TN_K + 2 * t + g, kT[0:QK, 4 * g:4 * g + 4, t * P:(t + 1) * P], 4, QK)
                heads = 2 * H1
                for s in range(heads + 2):
                    if s < H1:
                        shifts(s, scale=float(QK) ** -0.5)
                    elif s < heads:
                        dve.wait_ge(sem("alibi"), w.at("alibi", s - H1 + 1))
                        shifts(s, add=alibi[:, s % 2], scale=float(G_HD) ** -0.5, sink_h=s - H1)
                    if 1 <= s <= heads:
                        i = s - 1
                        normalise(i, ("score_read_a", i + 1) if i < H1 else ("expd", i - H1 + 1), i >= H1)
                    if s >= 2 and s % 2:
                        pair = (s - 2) // 2
                        j = pair % (H1 // 2)
                        hi, lo = (co_hi, co_lo) if pair < H1 // 2 else (oc_hi, oc_lo)
                        pair_lo(pair, lo[:, j, :], hi[:, j, :])
                    if s % 4 == 0 and s // 4 < FGROUPS:
                        tokens_lo(s // 4)
                    if s % 4 == 2 and s // 4 + 1 < FGROUPS:
                        width_lo(s // 4 + 1)
                split(1)
                for n, (gate_hf, hf, tiles) in enumerate(((HF_GB, HF_BB, 8), (HF_GA, HF_BA, 4), (HF_GC, HF_BC, 4))):
                    split(4 + tiles // 2 - 1)
                    for t in range(T):
                        half_there(hf + t)
                        _, name, k = w.read("half", gate_hf + t)
                        dve.wait_ge(sem(name), w.at(name, k))
                        dst = ht[:, t, :] if n == 0 else gate[:, t, :]
                        nc.vector.tensor_tensor(dst, gate[:, t, :], half_bank(hf + t, 2), ALU.mult)\
                            .then_inc(sem("half_read_v"), 1)
                        if n > 0:
                            _, name, k = w.read("half", hf + t)
                            dve.wait_ge(sem(name), w.at(name, k))
                            nc.vector.tensor_tensor(ht[:, t, :], ht[:, t, :], gate[:, t, :], ALU.add)\
                                .then_inc(sem(("merged", "h_ready")[n - 1]), 1)
                    split(1)
                turned_rows_lo(TN_MERGE)
                split(3)
                residual(6, 2, HF_OUT)
                split(1)
                for t in range(T):
                    dve.wait_ge(sem("x_ready"), w.at("x_ready", t + 1))
                    scaled(8 + t, 3, ht[:, t, :], xs[:, t, :]).then_inc(sem("h_ready"), 1)
                split(1)
                turned_rows_lo(TN_FFN)
                ffn(0, TN_HID)
                residual(10, 4, HF_DOWN)
                split(1)
                turned_rows_lo(TN_PLE)
                split(3)
                for t in range(T):
                    _, name, k = w.read("half", HF_PG + t)
                    dve.wait_ge(sem(name), w.at(name, k))
                    nc.vector.tensor_tensor(ht[:, t, :], ht[:, t, :], gate[:, t, :], ALU.mult)\
                        .then_inc(sem("e_ready"), 1)
                for t in range(T):
                    link(scaled(12 + t, 5, ht[:, t, :], ht[:, t, :]))
                    nc.vector.tensor_tensor(xs[:, t, :], xs[:, t, :], ht[:, t, :], ALU.add)\
                        .then_inc(sem("x_ready"), 1)
                split(1)

            def turn_of(i):
                return TN_HEAD + i if w.layer is not None else head_turns[i]

            n_setup = [0]

            def setup(ins):
                ins.then_inc(s_setup, 1)
                n_setup[0] += 1
                dve.wait_ge(s_setup, n_setup[0])

            dve.wait_ge(s_in["pos"], 64)
            words = T * (ROPE // 2)
            angle, turns_, near = (hid[:, 0, n * words:(n + 1) * words].rearrange("p (t f) -> p t f", t=T)
                                   for n in range(3))
            setup(nc.vector.tensor_copy(posf[:, 0, :], posq[:, :]))
            for t in range(T):
                setup(nc.vector.tensor_scalar(angle[:, t, :], freq[:, :], posf[:, 0, t:t + 1], None, ALU.mult))
            two_pi = 2 * math.pi
            part1 = 6.28125
            part2 = float(np.float32(math.floor((two_pi - part1) * 2.0 ** 21) / 2.0 ** 21))
            part3 = float(np.float32(two_pi - part1 - part2))
            magic = 1.5 * 2.0 ** 23
            for which in range(2):
                quarter = 0.25 if which == 0 else 0.0
                setup(nc.vector.tensor_scalar(turns_, angle, 1.0 / two_pi, quarter, ALU.mult, ALU.add))
                setup(nc.vector.tensor_scalar(turns_, turns_, magic, None, ALU.add))
                setup(nc.vector.tensor_scalar(turns_, turns_, magic, None, ALU.subtract))
                src = angle
                for part in (part1, part2, part3):
                    setup(nc.vector.scalar_tensor_tensor(near, turns_, -part, src, ALU.mult, ALU.add))
                    src = near
                setup(nc.vector.tensor_scalar(near, near, quarter * two_pi, 3.141592, ALU.add, ALU.min))
                setup(nc.vector.tensor_scalar(cs1[:, which], near, -3.141592, None, ALU.max))
            assert n_setup[0] == ANGLE_STEPS
            ki = h[:, 0:2 * S].bitcast(I32).rearrange("p (a n) -> p a n", a=2)
            kf = h[:, 2 * S:4 * S].rearrange("p (a n) -> p a n", a=2)
            df = h[:, 4 * S:6 * S].rearrange("p (t n) -> p t n", t=T)
            for src, dst in ((posk[:, :], ki), (posq[:, :], posi)):
                setup(nc.vector.tensor_scalar(dst[:, 0, :], src, 12, None, ALU.arith_shift_right))
                setup(nc.vector.tensor_scalar(dst[:, 1, :], src, 4095, None, ALU.bitwise_and))
            setup(nc.vector.tensor_copy(kf, ki))
            setup(nc.vector.tensor_copy(posf[:, 1:3, :], posi[:, :, :]))
            for t in range(T):
                setup(nc.vector.tensor_scalar(mask[:, t, :], kf[:, 0, :], posf[:, 1, t:t + 1], 4096.0,
                                              ALU.subtract, ALU.mult))
                setup(nc.vector.tensor_scalar(df[:, t, :], kf[:, 1, :], posf[:, 2, t:t + 1], None, ALU.subtract))
                setup(nc.vector.tensor_tensor(df[:, t, :], df[:, t, :], mask[:, t, :], ALU.add))
                setup(nc.vector.scalar_tensor_tensor(mask[:, t, :], df[:, t, :], -1.0, df[:, t, :],
                                                     ALU.mult, ALU.max))
            assert n_setup[0] == SETUP_STEPS
            half_hi = 0
            w.layer = 0
            split(SLOTS)
            with dve.Fori(0, DEPTH) as li:
                w.layer = li
                done[0], links[0], hi_n[0] = SLOTS, 0, 0
                layer1()
                assert done[0] == UNITS1 + SLOTS, done
                assert links[0] == PER_LAYER["v_link"], links
                assert hi_n[0] == PER_LAYER["turn_hi"], hi_n
            w.layer = None
            done[0], links[0], hi_n[0] = SLOTS, 0, 0

            n, tn, hf, gu = 0, 0, 0, 0
            head_turns = {}

            def norm_here():
                nonlocal n, tn
                for t in range(T):
                    scaled(n + t, n // 2, ht[:, t, :], xs[:, t, :]).then_inc(sem("h_ready"), 1)
                turned_rows_lo(tn)
                n, tn = n + T, tn + 4

            def add_here(scale=None):
                nonlocal hf
                for t in range(T):
                    half_there(hf + t)
                    if scale is None:
                        nc.vector.tensor_tensor(xs[:, t, :], xs[:, t, :], half_bank(hf + t, 2), ALU.add)\
                            .then_inc(sem("half_read_v"), 1)
                    else:
                        nc.vector.scalar_tensor_tensor(xs[:, t, :], half_bank(hf + t, 2), scale, xs[:, t, :],
                                                       ALU.mult, ALU.add).then_inc(sem("half_read_v"), 1)
                hf += T

            def ffn_here():
                nonlocal tn, gu
                norm_here()
                ffn(gu, tn)
                tn, gu = tn + 2 * NCH, gu + 2 * NCH
                add_here(0.5)
                split(1)

            def turn_keys():
                nonlocal tn
                for t in range(T):
                    for g in range(2):
                        turned_copy(tn + 2 * t + g, kT2[:, 4 * g:4 * g + 4, t * P:(t + 1) * P])
                tn += 4

            def attend(sc, mask_n):
                nonlocal tn
                dve.wait_ge(s_in["mask"], 16 * mask_n)
                for i in range(H2):
                    head_turns[sc + i] = tn + i
                for s in range(H2 + 2):
                    if s < H2:
                        shifts(sc + s, add=mask, scale=float(HD2) ** -0.5, causal=True)
                    if 1 <= s <= H2:
                        normalise(sc + s - 1, ("expd", sc + s), causal=True)
                    if s >= 2 and s % 2:
                        pair = (s - 2) // 2
                        pair_lo(sc // 2 + pair, o2_lo[:, pair, :], o2_hi[:, pair, :])
                tn += H2

            ffn_here()
            norm_here()
            split(12)
            hf += 3 * T
            tn += 4
            turn_keys()
            attend(0, 1)
            split(3)
            add_here()
            split(1)
            ffn_here()
            norm_here()
            split(8)
            hf += 2 * T
            turn_keys()
            ffn_here()
            norm_here()
            split(4)
            hf += T
            tn += 4
            attend(H2, 2)
            split(3)
            add_here()
            split(1)
            ffn_here()
            for t in range(T):
                scaled(n + t, n // 2, ht[:, t, :], xs[:, t, :]).then_inc(sem("result"), 1)

        @blk.gpsimd
        def _(pool):
            w = Place()
            links = [0]

            def link(ins):
                ins.then_inc(sem("g_link"), 1)
                links[0] += 1
                pool.wait_ge(sem("g_link"), w.at("g_link", links[0]))

            def inverse(n):
                pool.wait_ge(sem("squared"), w.at("squared", n + 1))
                link(nc.gpsimd.tensor_tensor(stat[:, n, 1:2], stat[:, n, 0:1], eps[:, :], ALU.add))
                nc.gpsimd.tensor_tensor(stat[:, n, 1:2], stat[:, n, 1:2], half_pow[:, :], ALU.pow)\
                    .then_inc(sem("inverse"), 1)

            def load_gain(row, slot, after=None):
                if after is not None:
                    pool.wait_ge(sem(after[0]), w.at(*after))
                pool.dma_start(gains[:, slot, :], A["gains"][bass.ds(row, 1), :].partition_broadcast(P)
                               .rearrange("p a n -> p (a n)")).then_inc(sem(f"gain_in{slot}"), 16)

            def rotate(src, dst, c, s, n_heads, half, ready):
                words = T * n_heads * half
                flat = alibi[:, :, :, :].rearrange("p a t n -> p (a t n)")
                prod = [flat[:, k * words:(k + 1) * words].rearrange("p (t h c) -> p t h c", t=T, h=n_heads)
                        for k in range(4)]
                shape = [P, T, n_heads, half]
                cb = c.unsqueeze(2).to_broadcast(shape)
                sb_ = s.unsqueeze(2).to_broadcast(shape)
                for k, (x, y) in enumerate(((src[0], cb), (src[1], sb_), (src[0], sb_), (src[1], cb))):
                    last = nc.gpsimd.tensor_tensor(prod[k], x, y, ALU.mult)
                link(last)
                a, b, c_, d = prod
                if dst[0].shape[2] != n_heads:
                    a, b, c_, d = (q.to_broadcast(list(dst[0].shape)) for q in prod)
                for t in range(T):
                    nc.gpsimd.tensor_tensor(dst[0][:, t], a[:, t], b[:, t], ALU.subtract)
                    last = nc.gpsimd.tensor_tensor(dst[1][:, t], c_[:, t], d[:, t], ALU.add)
                last.then_inc(sem(ready), 1)

            def layer1(li):
                pool.wait_ge(sem("pair_done"), w.at("pair_done", 0))
                pool.dma_start(probT[:, 0, :, :], A["p"][bass.ds(li, 1), 0, :, :]
                               .rearrange("a (t p) n -> p (a t) n", p=P)).then_inc(sem("aux_in"), 16)
                pool.dma_start(sink[:, :], A["gqa_sink"][bass.ds(li, 1), :].partition_broadcast(P)
                               .rearrange("p a n -> p (a n)")).then_inc(sem("aux_in"), 16)
                for t in range(T):
                    inverse(t)
                load_gain(li * 6 + 2, 0, ("h_ready", 2))
                for t in range(T):
                    inverse(2 + 2 * t)
                    inverse(3 + 2 * t)
                pool.wait_ge(sem("half_read_v"), w.at("half_read_v", HF_Z + 6))
                load_gain(li * 6 + 3, 1, ("c_ready", 2))
                nc.gpsimd.tensor_copy(vc[:, :, :], zs[:, :, Z_VC:Z_SMALL])
                nc.gpsimd.tensor_copy(kswap[:, :, 0:G_HD], zs[:, :, Z_KC + G_HD:Z_VC])
                nc.gpsimd.tensor_copy(kswap[:, :, G_HD:2 * G_HD], zs[:, :, Z_KC:Z_KC + G_HD])\
                    .then_inc(sem("kc_ready"), 1)
                r = ROPE // 2
                zr = zs[:, :, LORA:LORA + ROPE].unsqueeze(2)
                pool.wait_ge(sem("half_read_a"), w.at("half_read_a", 4))
                halves = (hq[:, :, :, NOPE:NOPE + r], hq[:, :, :, NOPE + r:QK])
                rotate(halves, halves, cs1[:, 0], cs1[:, 1], H1, r, "q_ready")
                pool.wait_ge(sem("q_ready"), w.at("q_ready", 1))
                rotate((zr[:, :, :, 0:r], zr[:, :, :, r:ROPE]),
                       (kfull[:, :, :, NOPE:NOPE + r], kfull[:, :, :, NOPE + r:QK]),
                       cs1[:, 0], cs1[:, 1], 1, r, "k_ready")
                pool.wait_ge(sem("k_ready"), w.at("k_ready", 1))
                for i in range(H1):
                    if i >= 2:
                        pool.wait_ge(sem("score_read_v"), w.at("score_read_v", i - 1))
                    nc.gpsimd.tensor_tensor(alibi[:, i % 2], mask[:, :, :],
                                            slopes[:, i:i + 1].unsqueeze(2).to_broadcast([P, T, S]),
                                            ALU.mult).then_inc(sem("alibi"), 1)
                for t in range(T):
                    inverse(6 + t)
                for t in range(T):
                    inverse(8 + t)
                load_gain(li * 6 + 4, 0, ("x_ready", 2))
                load_gain(li * 6 + 5, 1, ("h_ready", 6))
                for t in range(T):
                    inverse(10 + t)
                load_gain(li * 6 + 6, 0, ("x_ready", 4))
                for t in range(T):
                    inverse(12 + t)
                load_gain(li * 6 + 7, 1, ("x_ready", 6))

            n_setup = [0]

            def setup(ins):
                ins.then_inc(s_setup_g, 1)
                n_setup[0] += 1
                pool.wait_ge(s_setup_g, n_setup[0])

            nc.gpsimd.memset(half_pow[:, :], -0.5)
            nc.gpsimd.memset(eps[:, :], EPS)
            for i in range(H1):
                last = nc.gpsimd.memset(slopes[:, i:i + 1], -2.0 ** (-8.0 * (i + 1) / H1) * float(G_HD) ** 0.5)
            last.then_inc(s_ident, 1)
            setup(nc.gpsimd.memset(ident[:, :], 0.0))
            nc.gpsimd.affine_select(out=ident[:, :], in_=ident[:, :], compare_op=ALU.not_equal, fill=1.0,
                                    base=0, pattern=[[-1, P]], channel_multiplier=1).then_inc(s_ident, 1)
            load_gain(0, 0)
            load_gain(1, 1)
            pool.wait_ge(s_setup, SETUP_STEPS)
            setup(nc.gpsimd.affine_select(out=mask[:, 0, :], in_=mask[:, 0, :], compare_op=ALU.is_ge, fill=BIG,
                                          base=P, pattern=[[-1, S]], channel_multiplier=1))
            setup(nc.gpsimd.affine_select(out=mask[:, 1, :], in_=mask[:, 1, :], compare_op=ALU.is_ge, fill=BIG,
                                          base=0, pattern=[[1, S]], channel_multiplier=-1))
            pool.wait_ge(s_trig, 1)
            pool.wait_ge(s_ident, 2)
            with pool.Fori(0, DEPTH) as li:
                w.layer = li
                links[0] = 0
                layer1(li)
                assert links[0] == PER_LAYER["g_link"], links
            w.layer = None
            links[0] = 0

            n = 0
            first_row = 6 * DEPTH

            def norm_here():
                nonlocal n
                for t in range(T):
                    inverse(n + t)
                n += T
                if n // 2 + 1 < 8:
                    load_gain(first_row + n // 2 + 1, (n // 2 + 1) % 2, ("h_ready", n))

            def rotate_heads(buf, ready, after, n_ready):
                pool.wait_ge(sem("half_read_a"), w.at("half_read_a", after))
                v = buf[:, :, :].rearrange("p t (h c) -> p t h c", h=H2)
                halves = (v[:, :, :, 0:ROT // 2], v[:, :, :, ROT // 2:ROT])
                rotate(halves, halves, cs2[:, 0], cs2[:, 1], H2, ROT // 2, ready)
                pool.wait_ge(sem(ready), w.at(ready, n_ready))

            def load_mask(k):
                pool.dma_start(mask[:, :, :], A["masks"][k, :, :].rearrange("(t p) n -> p t n", p=P))\
                    .then_inc(s_in["mask"], 16)

            pool.wait_ge(s_in["const"], 16)
            pool.wait_ge(sem("alibi"), w.at("alibi", 0))
            load_mask(0)
            norm_here()
            norm_here()
            rotate_heads(q2, "q_ready", 2, 1)
            rotate_heads(k2, "k_ready", 4, 1)
            norm_here()
            load_mask(1)
            norm_here()
            rotate_heads(k2, "k_ready", 8, 2)
            norm_here()
            norm_here()
            rotate_heads(q2, "q_ready", 12, 2)
            norm_here()
            norm_here()


def host_constants():
    i = np.arange(S)
    angle = 2 * np.pi * (np.outer(i, i) % S) / S
    c, s = np.cos(angle) / 16.0, np.sin(angle) / 16.0
    dft = np.concatenate([c, -s, s], axis=1).astype(np.float32)
    half = ROPE // 2
    freq1 = (np.float32(THETA1) ** (-np.arange(half, dtype=np.float32) / np.float32(half)))
    freq1 = freq1.astype(np.float32).reshape(1, half)
    half = ROT // 2
    freq2 = (np.float32(THETA2) ** (-np.arange(half, dtype=np.float32) / np.float32(half))).astype(np.float32)
    ang2 = (np.arange(S, dtype=np.float32)[:, None] * freq2[None, :]).astype(np.float64)
    trig2 = np.stack([np.cos(ang2), np.sin(ang2)]).astype(np.float32)
    back = i[:, None] - i[None, :]
    count = np.zeros((S, S))
    for window, step in WINDOWS:
        count += (back >= 0) & (back <= window) & (back % step == 0)
    first = np.where(count > 0, np.log(np.maximum(count, 1)) * HD2 ** 0.5, -BIG)
    second = np.where(back >= 0, 0.0, -BIG)
    masks = np.stack([first, second]).astype(np.float32)
    return dict(dft=dft, freq1=freq1, trig2=trig2, masks=masks)


_WEIGHTS = ("w_in", "w_uq", "w_ukv", "w_branch_a", "w_branch_b", "w_branch_c", "w_out", "w_ffn_gate",
            "w_ffn_up", "w_ffn_down", "w_ple_proj", "w_ple_gate", "ffn1_w_gate_2", "ffn1_w_up_2",
            "ffn1_w_down_2", "ffn2_w_gate_2", "ffn2_w_up_2", "ffn2_w_down_2", "a_w_qkv_2", "a_w_o_2",
            "kv_w_2", "b_w_q_2", "b_w_o_2")


def device_arrays(inputs):
    arrays = {n: np.ascontiguousarray(inputs[n]) for n in ("x", "p", "positions", "gqa_sink", *_WEIGHTS)}
    rows = []
    for i in range(DEPTH):
        latent = np.zeros(D, np.float32)
        latent[0:Q_LORA] = inputs["mla_q_norm"][i]
        latent[Q_LORA:LORA] = inputs["mla_kv_norm"][i]
        rows += [inputs["norm_mix_pre"][i], latent, inputs["norm_mix_post"][i], inputs["norm_ffn_pre"][i],
                 inputs["norm_ffn_post"][i], inputs["norm_ple"][i]]
    for i in range(DEPTH):
        rows += [inputs["ffn1_norm_2"][i], inputs["mix_norm_2"][i], inputs["ffn2_norm_2"][i]]
        if i == 0:
            rows.append(inputs["kv_norm_2"])
    rows.append(inputs["final_norm_2"])
    arrays["gains"] = np.stack([np.asarray(r, np.float32) for r in rows])
    arrays.update(host_constants())
    return arrays


def kernel(**inputs):
    import concourse.bacc as bacc
    from concourse.bass_utils import run_bass_kernel_spmd

    nc = bacc.Bacc("TRN2", target_bir_lowering=False, num_devices=1)
    arrays = device_arrays({k: np.asarray(v) for k, v in inputs.items()})
    aps = {n: nc.dram_tensor(n + "_dram", a.shape, mybir.dt.from_np(a.dtype), kind="ExternalInput").ap()
           for n, a in arrays.items()}
    out = nc.dram_tensor("out_dram", (1, S, D), F32, kind="ExternalOutput").ap()
    two_blocks(nc, aps, out)
    result = run_bass_kernel_spmd(nc, [{n + "_dram": a for n, a in arrays.items()}], core_ids=[0])
    return result.results[0]["out_dram"]
```

```python
import math
from contextlib import ExitStack

import numpy as np

import concourse.bass as bass
from concourse import mybir

P = 128
S = 256
T = S // P
D = 1024
DT = D // P
DEPTH = 2
PLE = 256
EPS = 1e-6

H1 = 8
NOPE, ROPE, VD = 64, 32, 64
QK = NOPE + ROPE
Q_LORA, KV_LORA = 384, 128
LORA = Q_LORA + KV_LORA
G_HD, G_KV = 64, 2
THETA1 = 10000.0
FGROUPS = 4
FW = D // FGROUPS
Z_SMALL = LORA + ROPE + H1 * G_HD + 2 * G_KV * G_HD
Z_QC = LORA + ROPE
Z_KC = Z_QC + H1 * G_HD
Z_VC = Z_KC + G_KV * G_HD
Z_CUTS = (0, 512, 1024, Z_SMALL)
FFN = 2816
CH = 256
NCH = FFN // CH
H2, HD2, ROT = 16, 64, 16
THETA2 = 500000.0
WINDOWS = ((128, 1), (512, 4), (2048, 16))

SLOTS = 3
UW = 2048
BIG = 1e30
ANGLE_STEPS, SETUP_STEPS = 25, 31
PART_STEPS, DISTANCE_STEPS = 6, 10

F32 = mybir.dt.float32
F32R = mybir.dt.float32r
I32 = mybir.dt.int32
ALU = mybir.AluOpType
ACT = mybir.ActivationFunctionType
AX = mybir.AxisListType

U_Z, U_UQ, U_UKV, U_DFT = 0, 6, 8, 9
U_GATE_B, U_BR_B, U_GATE_A, U_BR_A, U_GATE_C, U_BR_C = 10, 14, 18, 22, 24, 28
U_OUT, U_PROJ, U_FFN, U_PGATE, UNITS1 = 30, 34, 35, 68, 72
UNITS_FFN = 3 * NCH

SPIN = "va"


def runs(*parts):
    return "".join(k * n for k, n in parts)


HALF1 = runs(("v", 6), ("a", 4), ("a", 2), ("v", 12), ("a", 4), ("v", 4), ("a", 2), ("v", 2),
             ("a", 2), ("v", 2), ("v", 2), ("a", 2), ("v", 2), ("a", 2))
HF_Z, HF_UQ, HF_UKV, HF_F, HF_GB, HF_BB, HF_GA, HF_BA, HF_GC, HF_BC, HF_OUT, HF_PROJ, HF_DOWN, HF_PG = (
    0, 6, 10, 12, 24, 28, 32, 34, 36, 38, 40, 42, 44, 46)
HALF2 = runs(("v", 2), ("a", 6), ("v", 2), ("v", 2), ("a", 4), ("v", 2), ("a", 2), ("v", 2), ("v", 2))
TURN1 = runs(("v", 4), ("v", 2), ("a", 2), ("v", 2), ("a", 4), ("v", 4), ("a", 16), ("v", 2),
             ("v", 4), ("v", 4), ("v", 2 * NCH), ("v", 4))
TN_MIX, TN_C, TN_QC, TN_KC, TN_Q, TN_K, TN_HEAD, TN_P, TN_MERGE, TN_FFN, TN_HID, TN_PLE = (
    0, 4, 6, 8, 10, 14, 18, 34, 36, 40, 44, 66)
TURN_FFN2 = ("v", 4 + 2 * NCH)
TURN2 = runs(TURN_FFN2, ("v", 4), ("a", 4), ("v", 4), ("a", 16), TURN_FFN2, ("v", 4),
             TURN_FFN2, ("v", 4), ("v", 4), ("a", 4), ("a", 16), TURN_FFN2)
SCORE1 = runs(("a", H1), ("v", H1))
SCORE2 = runs(("v", 2 * H2))
CLASSES = {
    "half": (HALF1, HALF2),
    "turn": (TURN1, TURN2),
    "score": (SCORE1, SCORE2),
    "gu": ("v" * (2 * NCH), "v" * (2 * NCH * 4)),
    "pair": ("v" * H1, "v" * H2),
}

PROBS = 3
WARM_SHORT, WARM_LONG = 8, 30
AHEAD_ONE, AHEAD_TWO = 6, 3

BASE = 1
BY_DMA = ("landed", "gain_in", "aux_in")

PER_LAYER = dict(
    landed=32 * UNITS1 // SLOTS, hi=UNITS1, lo=UNITS1,
    half_done=len(HALF1), turn_done=len(TURN1), score_done=2 * H1, gu_done=2 * NCH, pair_done=H1,
    half_hi=3 * FGROUPS, turn_hi=TURN1.count("v") - 6, pair_hi=H1,
    squared=14, inverse=14, gain_in=48, aux_in=32, silu=2 * NCH,
    h_ready=6, c_ready=2, x_ready=6, e_ready=2, merged=2,
    q_ready=1, k_ready=1, kc_ready=1, shift=2 * H1, expd=H1, probs=2 * H1, alibi=H1,
    v_link=34, g_link=16,
)
for _c, (_one, _) in CLASSES.items():
    for _e in SPIN:
        PER_LAYER[f"{_c}_read_{_e}"] = _one.count(_e)
PER_CHUNK = dict(landed=32, hi=3, lo=3, used=2, gu_done=2, gu_read_v=2, turn_done=2, turn_hi=2,
                 turn_read_v=2, silu=2)


def unit_ends():
    used = 0

    def plain(n):
        nonlocal used
        out = [("used", used + i + 1) for i in range(n)]
        used += n
        return out

    def wide(units, hf):
        return [*plain(units - 1), ("half_done", hf + 2)]

    def ffn(gu, hf):
        out = [*plain(1), ("gu_done", gu + 2)]
        for c in range(1, NCH):
            out += [*plain(1), ("gu_done", gu + 2 * c + 2), *plain(1)]
        return [*out, ("half_done", hf + 2)]

    one = []
    for c in range(3):
        one += [*plain(1), ("half_done", HF_Z + 2 * c + 2)]
    one += [("half_done", HF_UQ + 2), ("half_done", HF_UQ + 4), ("half_done", HF_UKV + 2)]
    one += [("half_done", HF_F + 3 * FGROUPS)]
    for c in range(4):
        one += [*plain(1), ("half_done", HF_GB + 2 * c + 2)]
    for units, hf in ((4, HF_GA), (2, HF_BA), (4, HF_GC), (2, HF_BC),
                      (4, HF_OUT), (1, HF_PROJ)):
        one += wide(units, hf)
    one += ffn(0, HF_DOWN) + wide(4, HF_PG)
    assert len(one) == UNITS1
    per_layer, used = used, 0
    two = ffn(0, 0)
    for n in range(4):
        two += wide(4, 2 + 2 * n)
    two += ffn(2 * NCH, 10) + wide(4, 12) + wide(4, 14) + ffn(4 * NCH, 16)
    two += wide(4, 18) + wide(4, 20) + ffn(6 * NCH, 22)
    return one, two, per_layer


ENDS1, ENDS2, PER_LAYER["used"] = unit_ends()


class Place:

    def __init__(self):
        self.layer = None
        self.chunk = None

    def at(self, name, n):
        key = {"landed": "landed", "gain_in": "gain_in"}.get(name.rstrip("0123456789"), name)
        per = PER_LAYER[key]
        if self.layer is None:
            v = DEPTH * per + n
        elif n >= 0:
            v = self.layer * per + n
        else:
            assert DEPTH == 2
            v = self.layer * (per + n)
        if self.chunk is not None:
            v = v + self.chunk * PER_CHUNK[key]
        return v if key in BY_DMA else v + BASE

    def read(self, cls, k):
        one, two = CLASSES[cls]
        if self.layer is None and k >= 0:
            return two[k], f"{cls}_read_{two[k]}", two[: k + 1].count(two[k])
        if k >= 0:
            return one[k], f"{cls}_read_{one[k]}", one[: k + 1].count(one[k])
        e = one[len(one) + k]
        return e, f"{cls}_read_{e}", one[: len(one) + k + 1].count(e) - one.count(e)

    def end_of(self, u):
        if self.layer is None and u >= 0:
            return ENDS2[u]
        if u >= 0:
            return ENDS1[u]
        name, n = ENDS1[UNITS1 + u]
        return name, n - PER_LAYER[name]


def two_blocks(nc, A, out):
    ctx = ExitStack()
    with ctx:
        def sb(name, shape, dt=F32):
            return ctx.enter_context(nc.sbuf_tensor(name, shape, dt))

        def under(name, shape, dt=F32):
            with nc.sbuf_tensor(name, shape, dt) as t:
                return t

        raw = sb("raw", [P, SLOTS, UW])
        whi = sb("whi", [P, SLOTS, UW], F32R)
        wlo = sb("wlo", [P, SLOTS, UW], F32R)
        xs = sb("xs", [P, T, D])
        h = sb("h", [P, T * D])
        act_hi = sb("act_hi", [P, DT, S], F32R)
        act_lo = sb("act_lo", [P, DT, S], F32R)
        gains = sb("gains", [P, 2, D])
        hid = sb("hid", [P, T, CH])
        hid_hi = sb("hid_hi", [P, CH // P, S], F32R)
        hid_lo = sb("hid_lo", [P, CH // P, S], F32R)
        prob = sb("prob", [P, PROBS, T, S])
        probT = sb("probT", [P, 2, T, S])
        ident = sb("ident", [P, P])
        mask = sb("mask", [P, T, S])
        alibi = sb("alibi", [P, 2, T, S])
        stat = sb("stat", [P, 16, 2])
        soft = sb("soft", [P, 5, 4, 2])
        sink = sb("sink", [P, H1])
        half_pow = sb("half_pow", [P, 1])
        eps = sb("eps", [P, 1])
        slopes = sb("slopes", [P, H1])
        cs1 = sb("cs1", [P, 2, T, ROPE // 2])
        cs2 = sb("cs2", [P, 2, T, ROT // 2])
        posk = sb("posk", [P, S], I32)
        posq = sb("posq", [P, T], I32)
        posi = sb("posi", [P, 2, T], I32)
        posf = sb("posf", [P, 3, T])
        freq = sb("freq", [P, ROPE // 2])

        block1 = ExitStack()
        with block1:
            def b1(name, shape, dt=F32):
                return block1.enter_context(nc.sbuf_tensor(name, shape, dt))

            kfull = under("kfull", [P, T, H1, QK])
            four_hi = b1("four_hi", [P, DT, S], F32R)
            four_lo = b1("four_lo", [P, DT, S], F32R)
            co_hi = b1("co_hi", [P, LORA // P, S], F32R)
            co_lo = b1("co_lo", [P, LORA // P, S], F32R)
            zs = under("zs", [P, T, Z_SMALL])
            oc_hi = b1("oc_hi", [P, H1 // 2, S], F32R)
            oc_lo = b1("oc_lo", [P, H1 // 2, S], F32R)
            b1("under_zs", [P, T * Z_SMALL - H1 * S])
            gate = under("gate", [P, T, D])
            fa_hi = b1("fa_hi", [P, T, 2 * FW], F32R)
            fa_lo = b1("fa_lo", [P, T, 2 * FW], F32R)
            v1 = b1("v1", [P, T, H1, VD])
            qT = b1("qT", [P, H1, S])
            kT = b1("kT", [P, H1, S])
            qcT = b1("qcT", [P, H1 // 2, S])
            kcT = b1("kcT", [P, 2, S])
            kswap = b1("kswap", [P, T, G_KV * G_HD])
            vc = b1("vc", [P, T, G_KV * G_HD])
        block2 = ExitStack()
        with block2:
            def b2(name, shape, dt=F32):
                return block2.enter_context(nc.sbuf_tensor(name, shape, dt))

            q2 = b2("q2", [P, T, D])
            k2 = b2("k2", [P, T, D])
            v2 = b2("v2", [P, T, D])
            qT2 = b2("qT2", [P, H2 // 2, S])
            kT2 = b2("kT2", [P, H2 // 2, S])
            o2_hi = b2("o2_hi", [P, DT, S], F32R)
            o2_lo = b2("o2_lo", [P, DT, S], F32R)

        ps = ctx.enter_context(nc.psum_tensor("ps", [P, 8, 512], F32))
        hq = h[:, 0:T * H1 * QK].rearrange("p (t h c) -> p t h c", t=T, h=H1)
        ht = h[:, :].rearrange("p (t n) -> p t n", t=T)
        junk = prob[:, :, :, :].rearrange("p a t n -> p (a t n)")

        dist_at = alibi[:, :, :, :].rearrange("p a t n -> p (a t n)")
        ki = dist_at[:, 0:2 * S].bitcast(I32).rearrange("p (a n) -> p a n", a=2)

        kf = probT[:, :, :, :].rearrange("p a t n -> p (a t n)")[:, 0:2 * S].rearrange("p (a n) -> p a n", a=2)
        df = dist_at[:, 2 * S:4 * S].rearrange("p (t n) -> p t n", t=T)

        sems = {}

        def sem(name):
            if name not in sems:
                sems[name] = ctx.enter_context(nc.semaphore(name))
            return sems[name]

        counted = [sem(name) for name in PER_LAYER if name not in BY_DMA]
        landed = [sem(f"landed{s}") for s in range(SLOTS)]
        s_in = {n: sem(f"in_{n}") for n in ("x", "pos", "const", "mask", "out")}
        s_setup = sem("setup")
        s_setup_g = sem("setup_g")
        s_parts = sem("parts")
        s_ident = sem("ident_ready")
        s_trig = sem("trig")
        blk = ctx.enter_context(nc.Block())

        def u_view(buf, u, kts, cols):
            return buf[:, u % SLOTS, 0:kts * cols].rearrange("p (k n) -> p k n", k=kts)

        def unit_words(u):
            if u < U_UQ:
                c = u // 2
                return 4 * (Z_CUTS[c + 1] - Z_CUTS[c])
            if u < U_UKV:
                return 3 * (H1 * QK // 2)
            return {U_UKV: 1024, U_DFT: 2 * 3 * S}.get(u, UW)

        @blk.sync
        def _(sp):
            w = Place()

            def load(u, parts):
                sp.wait_ge(sem("lo"), w.at("lo", u - SLOTS + 1))
                assert len(parts) == 2
                for dst, src in parts:
                    sp.dma_start(dst, src).then_inc(landed[u % SLOTS], 16)

            def block(name, li, k0, kts, n0, cols):
                src = A[name][bass.ds(li, 1), k0 * P:(k0 + kts) * P, n0:n0 + cols]
                return src.rearrange("a (k p) n -> p (a k) n", p=P)

            def wide(u, name, li, k0, n0=0):
                v = u_view(raw, u, 2, D)
                load(u, [(v[:, k:k + 1, :], block(name, li, k0 + k, 1, n0, D)) for k in range(2)])

            def ffn_units(u, names, li):
                wg, wu, wd = names

                def gu(u, k0, n0):
                    v = raw[:, u % SLOTS, :].rearrange("p (k g n) -> p k g n", k=4, g=2)
                    parts = []
                    for g, name in enumerate((wg, wu)):
                        src = A[name][bass.ds(li, 1), k0 * P:(k0 + 4) * P, bass.ds(n0, CH)]
                        parts.append((v[:, :, g, :], src.rearrange("a (k p) n -> p (a k) n", p=P)))
                    load(u, parts)

                def down(u, row0):
                    v = u_view(raw, u, 2, D)
                    parts = []
                    for k in range(2):
                        src = A[wd][bass.ds(li, 1), bass.ds(row0 + k * P, P), :]
                        parts.append((v[:, k, :], src.rearrange("a p n -> p (a n)")))
                    load(u, parts)

                gu(u, 0, 0)
                gu(u + 1, 4, 0)
                gu(u + 2, 0, CH)
                gu(u + 3, 4, CH)
                down(u + 4, 0)
                with sp.Fori(0, NCH - 3) as i:
                    w.chunk = i
                    gu(u + 5, 0, i * CH + 2 * CH)
                    gu(u + 6, 4, i * CH + 2 * CH)
                    down(u + 7, i * CH + CH)
                w.chunk = None
                last = u + UNITS_FFN - 4
                gu(last, 0, (NCH - 1) * CH)
                gu(last + 1, 4, (NCH - 1) * CH)
                down(last + 2, (NCH - 2) * CH)
                down(last + 3, (NCH - 1) * CH)

            sp.dma_start(xs[:, :, :], A["x"][0, :, :].rearrange("(t p) n -> p t n", p=P)).then_inc(s_in["x"], 16)
            with sp.Fori(0, DEPTH) as li:
                w.layer = li
                for c in range(3):
                    n0, cols = Z_CUTS[c], Z_CUTS[c + 1] - Z_CUTS[c]
                    for j in range(2):
                        v = u_view(raw, 2 * c + j, 4, cols)
                        load(2 * c + j, [(v[:, k:k + 2, :], block("w_in", li, 4 * j + k, 2, n0, cols)) for k in (0, 2)])
                for j in range(2):
                    cols = H1 * QK // 2
                    v = u_view(raw, U_UQ + j, 3, cols)
                    load(U_UQ + j, [(v[:, 0:2, :], block("w_uq", li, 0, 2, j * cols, cols)),
                                    (v[:, 2:3, :], block("w_uq", li, 2, 1, j * cols, cols))])
                v = u_view(raw, U_UKV, 1, D)
                load(U_UKV, [(v[:, :, n:n + 512], block("w_ukv", li, 0, 1, n, 512)) for n in (0, 512)])
                v = u_view(raw, U_DFT, 2, 3 * S)
                load(U_DFT, [(v[:, k, :], A["dft"][k * P:(k + 1) * P, :]) for k in range(2)])
                for u0, name, first in ((U_GATE_B, "w_in", Z_SMALL + D), (U_BR_B, "w_branch_b", 0)):
                    for u in range(4):
                        v = u_view(raw, u0 + u, 4, D // 2)
                        load(u0 + u, [(v[:, k:k + 2, :], block(name, li, 4 * (u % 2) + k, 2,
                                                              first + u // 2 * (D // 2), D // 2))
                                      for k in (0, 2)])
                for u0, g0, br, name, tiles in ((U_GATE_A, 0, U_BR_A, "w_branch_a", 4),
                                                (U_GATE_C, 2, U_BR_C, "w_branch_c", 4)):
                    for j in range(4):
                        wide(u0 + j, "w_in", li, 2 * j, Z_SMALL + g0 * D)
                    for j in range(tiles // 2):
                        wide(br + j, name, li, 2 * j)
                for j in range(4):
                    wide(U_OUT + j, "w_out", li, 2 * j)
                wide(U_PROJ, "w_ple_proj", li, 0)
                ffn_units(U_FFN, ("w_ffn_gate", "w_ffn_up", "w_ffn_down"), li)
                for j in range(4):
                    wide(U_PGATE + j, "w_ple_gate", li, 2 * j)
            w.layer = None
            u = 0
            ffn1 = ("ffn1_w_gate_2", "ffn1_w_up_2", "ffn1_w_down_2")
            ffn2 = ("ffn2_w_gate_2", "ffn2_w_up_2", "ffn2_w_down_2")
            ffn_units(u, ffn1, 0)
            u += UNITS_FFN
            for n in range(3):
                for j in range(4):
                    wide(u + j, "a_w_qkv_2", 0, 2 * j, n * D)
                u += 4
            for j in range(4):
                wide(u + j, "a_w_o_2", 0, 2 * j)
            u += 4
            ffn_units(u, ffn2, 0)
            u += UNITS_FFN
            for n in range(2):
                for j in range(4):
                    v = u_view(raw, u + j, 2, D)
                    load(u + j, [(v[:, k, :], A["kv_w_2"][(2 * j + k) * P:(2 * j + k + 1) * P, n * D:(n + 1) * D])
                                 for k in range(2)])
                u += 4
            ffn_units(u, ffn1, 1)
            u += UNITS_FFN
            for name in ("b_w_q_2", "b_w_o_2"):
                for j in range(4):
                    wide(u + j, name, 0, 2 * j)
                u += 4
            ffn_units(u, ffn2, 1)
            for t in range(T):
                sp.wait_ge(sem("result"), t + 1)
                sp.dma_start(out[0, t * P:(t + 1) * P, :], ht[:, t, :]).then_inc(s_in["out"], 16)
            sp.wait_ge(s_in["out"], 16 * T)

        @blk.tensor
        def _(pe):
            w = Place()

            def free_before(cls, k):
                _, name, n = w.read(cls, k - 2)
                pe.wait_ge(sem(name), w.at(name, n))

            def was_read(cls, k):
                _, name, n = w.read(cls, k)
                pe.wait_ge(sem(name), w.at(name, n))

            def unit_there(u):
                pe.wait_ge(sem("lo"), w.at("lo", u + 1))

            def product(outs, hi, lo, whs, wls, start, stop):
                for o, a in zip(outs, whs):
                    nc.tensor.matmul(o, hi, a, start=start, stop=False)
                for o, a in zip(outs, wls):
                    nc.tensor.matmul(o, hi, a, start=False, stop=False)
                for o, a in zip(outs, whs):
                    last = nc.tensor.matmul(o, lo, a, start=False, stop=stop)
                return last

            def turn(k, src, n, rows=P, dst=None):
                free_before("turn", k)
                bank = ps[:, 2 + k % 2, :]
                for j in range(n):
                    last = nc.tensor.transpose(bank[0:rows, j * P:(j + 1) * P], src(j), ident[:, :])
                last.then_inc(sem("turn_done"), 1)

            def stay_warm(k, n):
                free_before("turn", k)
                for _ in range(n):
                    nc.tensor.transpose(ps[:, 2 + k % 2, 0:P], ident[:, :], ident[:, :])

            def rows(k, name, n, src=None, ahead=AHEAD_TWO):
                src = ht if src is None else src
                turned = [False, False]

                def turn_tile(t):
                    if not turned[t]:
                        turned[t] = True
                        pe.wait_ge(sem(name), w.at(name, n + t + 1))
                        for g in range(2):
                            turn(k + 2 * t + g, lambda j: src[:, t, (4 * g + j) * P:(4 * g + j + 1) * P], 4)

                def ready(t, kt):
                    if kt in (0, ahead):
                        turn_tile(0 if (t, kt) == (0, 0) else 1)
                    if kt % 4 == 0:
                        was_read("turn", k + 2 * t + kt // 4)
                return ready, turn_tile

            def wide_job(u, units, hf, hi, lo, ready=None, late=None):
                for j0 in range(0, units, 2):
                    for t in range(T):
                        for j in range(j0, min(j0 + 2, units)):
                            if t == 0:
                                unit_there(u + j)
                            if j == 0:
                                free_before("half", hf + t)
                            if late and (j, t) == (units - 1, T - 1):
                                late()
                            vh, vl = u_view(whi, u + j, 2, D), u_view(wlo, u + j, 2, D)
                            for k in range(2):
                                kt = 2 * j + k
                                if ready is not None:
                                    ready(t, kt)
                                outs = [ps[:, 4 + 2 * t + n, :] for n in range(2)]
                                last = product(outs, hi[:, kt, t * P:(t + 1) * P], lo[:, kt, t * P:(t + 1) * P],
                                               [vh[:, k, n * 512:(n + 1) * 512] for n in range(2)],
                                               [vl[:, k, n * 512:(n + 1) * 512] for n in range(2)],
                                               j == 0 and k == 0, j == units - 1 and k == 1)
                            if j == units - 1:
                                last.then_inc(sem("half_done"), 1)
                            elif t == T - 1:
                                last.then_inc(sem("used"), 1)

            def ffn(u, gu, tn, hf, ready):
                def gate_up(u, gu, ready=None):
                    def tile(t):
                        free_before("gu", gu + t)
                        for j in range(2):
                            if t == 0:
                                unit_there(u + j)
                            vh, vl = u_view(whi, u + j, 4, 512), u_view(wlo, u + j, 4, 512)
                            for k in range(4):
                                kt = 4 * j + k
                                if ready is not None:
                                    ready(t, kt)
                                last = product([ps[:, t, :]], act_hi[:, kt, t * P:(t + 1) * P],
                                               act_lo[:, kt, t * P:(t + 1) * P],
                                               [vh[:, k, :]], [vl[:, k, :]], kt == 0, kt == DT - 1)
                            if t == T - 1 and j == 0:
                                last.then_inc(sem("used"), 1)
                        last.then_inc(sem("gu_done"), 1)
                    return tile

                def turn_hidden(n, tn, tiles=range(T)):
                    for t in tiles:
                        pe.wait_ge(sem("gu_read_v"), w.at("gu_read_v", n + t + 1))
                        turn(tn + t, lambda j: hid[:, t, j * P:(j + 1) * P], CH // P)

                def down(u, tn, tiles=range(T), start=False, stop=False):
                    unit_there(u)
                    vh, vl = u_view(whi, u, 2, D), u_view(wlo, u, 2, D)
                    for t in tiles:
                        if start:
                            free_before("half", hf + t)
                        was_read("turn", tn + t)
                        for k in range(2):
                            outs = [ps[:, 4 + 2 * t + n, :] for n in range(2)]
                            last = product(outs, hid_hi[:, k, t * P:(t + 1) * P], hid_lo[:, k, t * P:(t + 1) * P],
                                           [vh[:, k, n * 512:(n + 1) * 512] for n in range(2)],
                                           [vl[:, k, n * 512:(n + 1) * 512] for n in range(2)],
                                           start and k == 0, stop and k == 1)
                        if stop:
                            last.then_inc(sem("half_done"), 1)
                    if not stop and t == T - 1:
                        last.then_inc(sem("used"), 1)

                def chunk(u, gu, tn, start):
                    tile = gate_up(u, gu)
                    tile(0)
                    turn_hidden(gu - T, tn)
                    tile(1)
                    down(u + 2, tn, start=start)

                tile = gate_up(u, gu, ready)
                tile(0)
                tile(1)
                chunk(u + 2, gu + 2, tn, True)
                with pe.Fori(0, NCH - 3) as i:
                    w.chunk = i
                    chunk(u + 5, gu + 4, tn + 2, False)
                w.chunk = None
                u, gu, tn = u + UNITS_FFN - 4, gu + 2 * (NCH - 1), tn + 2 * (NCH - 1)
                turn_hidden(gu - T, tn - T)
                tile = gate_up(u, gu)
                tile(0)
                down(u + 2, tn - T, tiles=(0,))
                turn_hidden(gu, tn, tiles=(0,))
                tile(1)
                down(u + 2, tn - T, tiles=(1,))
                turn_hidden(gu, tn, tiles=(1,))
                down(u + 3, tn, stop=True)

            def head(i, sc, tn, q, k, v, causal):
                rows = q[0].shape[0]

                def score():
                    free_before("score", sc)
                    for t in range(T):
                        cols = (t + 1) * P if causal else S
                        last = nc.tensor.matmul(ps[:, sc % 2, t * S:t * S + cols], q[t], k[:, 0:cols],
                                                start=True, stop=True)
                    last.then_inc(sem("score_done"), 1)

                def turn_probs():
                    free_before("turn", tn)
                    pe.wait_ge(sem("probs"), w.at("probs", sc + 1))
                    for kt in range(T):
                        for t in range(kt if causal else 0, T):
                            last = nc.tensor.transpose(ps[:, 2 + tn % 2, kt * S + t * P:kt * S + (t + 1) * P],
                                                       prob[:, sc % PROBS, t, kt * P:(kt + 1) * P], ident[:, :])
                    last.then_inc(sem("turn_done"), 1)

                def output():
                    pair, odd = sc // 2, sc % 2
                    if not odd:
                        free_before("pair", pair)
                    was_read("turn", tn)
                    o = ps[VD * odd:VD * (odd + 1), 5 + 2 * (pair % 2), :]
                    for kt in range(T):
                        c0 = kt * P if causal else 0
                        last = nc.tensor.matmul(o[:, c0:S], v[:, kt], probT[:, sc % 2, kt, c0:S],
                                                start=kt == 0, stop=kt == T - 1)
                    if odd:
                        last.then_inc(sem("pair_done"), 1)

                return score, turn_probs, output

            def attend(heads, scored, values):
                n = len(heads)
                for s in range(n):
                    for i in (s, s + 1) if s == 0 else (s + 1,):
                        if scored <= i < n:
                            heads[i][0]()
                    if s == 2:
                        was_read("half", values)
                    if s >= 2:
                        heads[s - 2][2]()
                    if s >= 1:
                        heads[s - 1][1]()

            def attend_beside(heads, others):
                n = len(heads)
                assert len(others) == n
                heads[0][0]()
                others[0]()
                for s in range(n):
                    if s + 1 < n:
                        heads[s + 1][0]()
                    if s > 0:
                        heads[s - 1][2]()
                    heads[s][1]()
                    if s + 1 < n:
                        others[s + 1]()

            def halves2(pT):
                return [pT[:, t * P:(t + 1) * P] for t in range(T)]

            def layer1():
                ready, turn_first = rows(TN_MIX, "h_ready", 0, ahead=AHEAD_ONE)
                turn_first(0)
                for c in range(3):
                    cols = Z_CUTS[c + 1] - Z_CUTS[c]
                    for t in range(T):
                        if (c, t) == (2, 1):
                            for tc in range(T):
                                pe.wait_ge(sem("c_ready"), w.at("c_ready", tc + 1))
                                turn(TN_C + tc, lambda j: zs[:, tc, j * P:(j + 1) * P], LORA // P)
                        free_before("half", HF_Z + 2 * c + t)
                        for j in range(2):
                            u = U_Z + 2 * c + j
                            if t == 0:
                                unit_there(u)
                            vh, vl = u_view(whi, u, 4, cols), u_view(wlo, u, 4, cols)
                            for k in range(4):
                                kt = 4 * j + k
                                if c == 0:
                                    ready(t, kt)
                                last = product([ps[:, 4 + 2 * t, 0:cols]], act_hi[:, kt, t * P:(t + 1) * P],
                                               act_lo[:, kt, t * P:(t + 1) * P],
                                               [vh[:, k, :]], [vl[:, k, :]], kt == 0, kt == DT - 1)
                            if t == T - 1 and j == 0:
                                last.then_inc(sem("used"), 1)
                        last.then_inc(sem("half_done"), 1)
                cols = H1 * QK // 2
                for j in range(2):
                    u = U_UQ + j
                    unit_there(u)
                    vh, vl = u_view(whi, u, 3, cols), u_view(wlo, u, 3, cols)
                    for t in range(T):
                        free_before("half", HF_UQ + 2 * j + t)
                        if j == 0:
                            was_read("turn", TN_C + t)
                        for k in range(3):
                            last = product([ps[:, 4 + 2 * t, 0:cols]], co_hi[:, k, t * P:(t + 1) * P],
                                           co_lo[:, k, t * P:(t + 1) * P], [vh[:, k, :]], [vl[:, k, :]],
                                           k == 0, k == 2)
                        last.then_inc(sem("half_done"), 1)
                was_read("half", HF_Z + 5)
                for t in range(T):
                    turn(TN_QC + t, lambda j: zs[:, t, Z_QC + j * P:Z_QC + (j + 1) * P], H1 // 2)
                pe.wait_ge(sem("kc_ready"), w.at("kc_ready", 1))
                for t in range(T):
                    turn(TN_KC + t, lambda j: (zs[:, t, Z_KC:Z_KC + P], kswap[:, t, :])[j], 2)
                unit_there(U_UKV)
                vh, vl = u_view(whi, U_UKV, 1, D), u_view(wlo, U_UKV, 1, D)
                for t in range(T):
                    free_before("half", HF_UKV + t)
                    last = product([ps[:, 4 + 2 * t + n, :] for n in range(2)],
                                   co_hi[:, 3, t * P:(t + 1) * P], co_lo[:, 3, t * P:(t + 1) * P],
                                   [vh[:, 0, n * 512:(n + 1) * 512] for n in range(2)],
                                   [vl[:, 0, n * 512:(n + 1) * 512] for n in range(2)], True, True)
                    last.then_inc(sem("half_done"), 1)

                dh, dl = u_view(whi, U_DFT, 2, 3 * S), u_view(wlo, U_DFT, 2, 3 * S)

                def over_width(g):
                    for t in range(T):
                        hf = HF_F + 3 * g + t
                        free_before("half", hf)
                        for k in range(2):
                            last = product([ps[:, 4 + 2 * (hf % 2), :]], act_hi[:, 2 * g + k, t * P:(t + 1) * P],
                                           act_lo[:, 2 * g + k, t * P:(t + 1) * P],
                                           [dh[:, k, 0:2 * S]], [dl[:, k, 0:2 * S]], k == 0, k == 1)
                        last.then_inc(sem("half_done"), 1)

                def over_tokens(g):
                    hf = HF_F + 3 * g + 2
                    free_before("half", hf)
                    for t in range(T):
                        was_read("half", HF_F + 3 * g + t)
                    for j in range(2):
                        for t in range(T):
                            for part, c0 in ((0, 0), (1, 2 * S)):
                                a = part * FW + j * P
                                last = product([ps[:, 4 + 2 * (hf % 2), j * S:(j + 1) * S]],
                                               fa_hi[:, t, a:a + P], fa_lo[:, t, a:a + P],
                                               [dh[:, t, c0:c0 + S]], [dl[:, t, c0:c0 + S]],
                                               t == 0 and part == 0, t == T - 1 and part == 1)
                    last.then_inc(sem("half_done"), 1)

                unit_there(U_DFT)
                over_width(0)
                pe.wait_ge(sem("q_ready"), w.at("q_ready", 1))
                for t in range(T):
                    for g in range(2):
                        turn(TN_Q + 2 * t + g, lambda j: hq[:, t, 4 * g + j, :], 4, QK)
                pe.wait_ge(sem("k_ready"), w.at("k_ready", 1))
                was_read("half", HF_UKV + 1)
                for t in range(T):
                    for g in range(2):
                        turn(TN_K + 2 * t + g, lambda j: kfull[:, t, 4 * g + j, :], 4, QK)
                for k in (TN_QC + 1, TN_KC + 1, TN_Q + 3, TN_K + 3):
                    was_read("turn", k)
                heads = []
                for i in range(H1):
                    heads.append(head(i, i, TN_HEAD + i, halves2(qT[0:QK, i, :]), kT[0:QK, i, :],
                                      v1[:, :, i, :], False))
                for i in range(H1):
                    n, odd = i // (H1 // G_KV), i % 2
                    part = slice(G_HD * odd, G_HD * (odd + 1))
                    heads.append(head(i, H1 + i, TN_HEAD + H1 + i, halves2(qcT[part, i // 2, :]),
                                      kcT[part, 0 if n == odd else 1, :],
                                      vc[:, :, n * G_HD:(n + 1) * G_HD], False))
                def half_job(i, hi, lo, tiles=range(T)):
                    u, c, j = U_GATE_B + i, i // 2, i % 2
                    unit_there(u)
                    vh, vl = u_view(whi, u, 4, D // 2), u_view(wlo, u, 4, D // 2)
                    for t in tiles:
                        hf = HF_GB + 2 * c + t
                        if j == 0:
                            free_before("half", hf)
                        for k in range(4):
                            last = product([ps[:, 4 + 2 * t, :]], hi[:, 4 * j + k, t * P:(t + 1) * P],
                                           lo[:, 4 * j + k, t * P:(t + 1) * P],
                                           [vh[:, k, :]], [vl[:, k, :]], 4 * j + k == 0, 4 * j + k == DT - 1)
                        if j == 1:
                            last.then_inc(sem("half_done"), 1)
                    if j == 0:
                        last.then_inc(sem("used"), 1)

                others = [lambda: over_tokens(0)]
                for g in range(1, FGROUPS):
                    others += [lambda g=g: over_width(g), lambda g=g: over_tokens(g)]
                others += [lambda i=i: half_job(i, act_hi, act_lo) for i in range(4)]
                branch = [lambda i=i: half_job(i, four_hi, four_lo) for i in range(4, 7)]
                branch += [lambda t=t: half_job(7, four_hi, four_lo, (t,)) for t in range(T)]

                def first_branch():
                    was_read("half", HF_F + 3 * FGROUPS - 1)
                    branch[0]()

                others += [first_branch, *branch[1:]]
                attend_beside(heads, others)

                def after_heads(t, kt):
                    if (t, kt) == (0, 1):
                        heads[-1][2]()
                    if kt == 0:
                        was_read("pair", H1 - T + t)

                wide_job(U_GATE_A, 4, HF_GA, act_hi, act_lo, after_heads)
                wide_job(U_BR_A, 2, HF_BA, co_hi, co_lo)
                wide_job(U_GATE_C, 4, HF_GC, act_hi, act_lo)
                pe.wait_ge(sem("aux_in"), w.at("aux_in", 32))
                for t in range(T):
                    turn(TN_P + t, lambda j: probT[:, 0, t, j * P:(j + 1) * P], PLE // P)
                merged, turn_merged = rows(TN_MERGE, "h_ready", 2)
                wide_job(U_BR_C, 2, HF_BC, oc_hi, oc_lo, late=lambda: turn_merged(0))
                wide_job(U_OUT, 4, HF_OUT, act_hi, act_lo, merged)
                for t in range(T):
                    was_read("turn", TN_P + t)
                wide_job(U_PROJ, 1, HF_PROJ, hid_hi, hid_lo)
                ffn(U_FFN, 0, TN_HID, HF_DOWN, rows(TN_FFN, "h_ready", 4, ahead=AHEAD_ONE)[0])
                stay_warm(TN_PLE, WARM_SHORT)
                wide_job(U_PGATE, 4, HF_PG, act_hi, act_lo, rows(TN_PLE, "x_ready", 2, xs)[0])
                stay_warm(len(TURN1) + TN_MIX, WARM_LONG)

            for s in counted:
                pe.sem_inc(s, BASE)
            pe.wait_ge(s_ident, 2)
            with pe.Fori(0, DEPTH) as li:
                w.layer = li
                layer1()
            w.layer = None

            u, gu, tn, hf, hr = 0, 0, 0, 0, 0

            def h_rows(ahead=AHEAD_TWO):
                nonlocal tn, hr
                hr += 2
                tn += 4
                return rows(tn - 4, "h_ready", hr - 2, ahead=ahead)[0]

            def ffn_here():
                nonlocal u, gu, tn, hf
                ready = h_rows(AHEAD_ONE)
                ffn(u, gu, tn, hf, ready)
                u, gu, tn, hf = u + UNITS_FFN, gu + 2 * NCH, tn + 2 * NCH, hf + 2
                if tn < len(TURN2):
                    stay_warm(tn, WARM_SHORT)

            def wide_here(hi, lo, ready=None):
                nonlocal u, hf
                wide_job(u, 4, hf, hi, lo, ready)
                u, hf = u + 4, hf + 2

            def head_turner(name, n, src):
                nonlocal tn
                base = tn
                tn += 4

                def turn_heads(e):
                    t, g = e // 2, e % 2
                    if g == 0:
                        pe.wait_ge(sem(name), w.at(name, T * (n - 1) + t + 1))
                    turn(base + e, lambda j: src[:, t, (4 * g + j) * P:(4 * g + j + 1) * P], 4)
                return turn_heads, base + 3

            def beside(steps, ready=None):
                def call(t, kt):
                    if ready is not None:
                        ready(t, kt)
                    if (t, kt) in steps:
                        steps[t, kt]()
                return call

            def heads_here(sc):
                nonlocal tn
                heads = []
                for i in range(H2):
                    part = slice(HD2 * (i % 2), HD2 * (i % 2 + 1))
                    heads.append(head(i, sc + i, tn + i, halves2(qT2[part, i // 2, :]), kT2[part, i // 2, :],
                                      v2[:, :, i * HD2:(i + 1) * HD2], True))
                tn += H2
                return heads

            def output_job(heads, pair):
                def last_turn():
                    heads[-2][2]()
                    heads[-1][1]()

                wide_here(o2_hi, o2_lo, beside({
                    (0, 0): lambda: was_read("pair", pair - 1), (0, 1): last_turn, (0, 2): heads[-1][2],
                    (1, 0): lambda: was_read("pair", pair)}))

            ffn_here()
            wide_here(act_hi, act_lo, h_rows())
            turn_q, last_q = head_turner("q_ready", 1, q2)
            wide_here(act_hi, act_lo, beside({(0, 4 + e): lambda e=e: turn_q(e) for e in range(4)}))
            turn_k, last_k = head_turner("k_ready", 1, k2)
            heads = heads_here(0)

            def first_score():
                for k in (last_q - 1, last_q, last_k - 1, last_k):
                    was_read("turn", k)
                heads[0][0]()

            steps = {(0, 4 + e): lambda e=e: turn_k(e) for e in range(4)}
            steps.update({(1, 5): first_score, (1, 6): heads[1][0]})
            wide_here(act_hi, act_lo, beside(steps))
            attend(heads, 2, hf - 1)
            output_job(heads, H2 // 2 - 1)
            ffn_here()
            wide_here(act_hi, act_lo, h_rows())
            wide_here(act_hi, act_lo)
            values_read = hf - 1
            ffn_here()
            ready = h_rows()
            turn_k, last_k = head_turner("k_ready", 2, k2)
            wide_here(act_hi, act_lo, beside({(1, 4 + e): lambda e=e: turn_k(e) for e in range(4)}, ready))
            turn_q, last_q = head_turner("q_ready", 2, q2)
            for e in range(4):
                turn_q(e)
            heads = heads_here(H2)
            for k in (last_k - 1, last_k, last_q - 1, last_q):
                was_read("turn", k)
            attend(heads, 0, values_read)
            output_job(heads, H2 - 1)
            ffn_here()

        def stat_of(w, n):
            return n % PER_LAYER["squared"] if w.layer is not None else n

        def soft_of(i):
            return [soft[:, n, i % 4, :] for n in range(5)]

        @blk.scalar
        def _(act):
            w = Place()
            done = [0]

            def split(n):
                for _ in range(n):
                    u = done[0]
                    if w.layer is None and u == len(ENDS2):
                        return
                    act.wait_ge(landed[u % SLOTS], w.at(f"landed{u % SLOTS}", 32 * (u // SLOTS + 1)))
                    if not at_start:
                        name, k = w.end_of(u - SLOTS)
                        act.wait_ge(sem(name), w.at(name, k))
                    words = unit_words(u) if w.layer is not None else UW
                    nc.scalar.activation(whi[:, u % SLOTS, 0:words], raw[:, u % SLOTS, 0:words], ACT.Copy)\
                        .then_inc(sem("hi"), 1)
                    done[0] += 1

            def turned_hi(k, dst, n=4):
                act.wait_ge(sem("turn_done"), w.at("turn_done", k + 1))
                nc.scalar.activation(dst, ps[:, 2 + k % 2, 0:n * P].rearrange("p (j c) -> p j c", j=n),
                                     ACT.Copy).then_inc(sem("turn_hi"), 1)

            def turned_copy(k, dst, n=4, rows=P):
                act.wait_ge(sem("turn_done"), w.at("turn_done", k + 1))
                nc.scalar.activation(dst, ps[0:rows, 2 + k % 2, 0:n * P].rearrange("p (j c) -> p j c", j=n),
                                     ACT.Copy).then_inc(sem("turn_read_a"), 1)

            def turned_rows_hi(k, tiles=range(T)):
                for t in tiles:
                    for g in range(2):
                        turned_hi(k + 2 * t + g, act_hi[:, 4 * g:4 * g + 4, t * P:(t + 1) * P])

            def half_there(hf):
                act.wait_ge(sem("half_done"), w.at("half_done", hf + 1))

            def half_bank(hf, banks=1):
                return ps[:, 4 + 2 * (hf % 2):4 + 2 * (hf % 2) + banks, :].rearrange("p b n -> p (b n)")

            def square(n, src):
                words = src.shape[-1]
                act.wait_ge(sem("squared"), w.at("squared", n))
                nc.scalar.activation(junk[:, 0:words], src, ACT.Square, scale=float(words) ** -0.5,
                                     accum_out=stat[:, stat_of(w, n), 0:1])\
                    .then_inc(sem("squared"), 1)

            def ffn(gu, tn, silu_n):
                def silu(gu, t, tn=None):
                    act.wait_ge(sem("gu_done"), w.at("gu_done", gu + t + 1))
                    if tn is not None:
                        act.wait_ge(sem("turn_done"), w.at("turn_done", tn + t + 1))
                    nc.scalar.activation(hid[:, t, :], ps[:, t, 0:CH], ACT.Silu).then_inc(sem("silu"), 1)

                def hidden_hi(tn, tiles=range(T)):
                    for t in tiles:
                        turned_hi(tn + t, hid_hi[:, :, t * P:(t + 1) * P], CH // P)

                def chunk(gu, tn):
                    silu(gu, 0, tn)
                    hidden_hi(tn)
                    split(1)
                    silu(gu, 1, tn)
                    split(2)

                silu(gu, 0)
                split(1)
                silu(gu, 1)
                split(1)
                chunk(gu + 2, tn)
                with act.Fori(0, NCH - 3) as i:
                    w.chunk = i
                    chunk(gu + 4, tn + 2)
                w.chunk = None
                done[0] += 3 * (NCH - 4)
                last = NCH - 1
                gu, tn = gu + 2 * last, tn + 2 * last
                hidden_hi(tn - T)
                silu(gu, 0, tn - T)
                hidden_hi(tn, (0,))
                split(1)
                silu(gu, 1, tn - T)
                split(1)
                hidden_hi(tn, (1,))
                split(1)

            def exps(i, scale=None, sink_h=None, causal=False):
                _, nm, sm, _, es = soft_of(i)
                if causal:
                    _, name, k = w.read("score", i)
                    act.wait_ge(sem(name), w.at(name, k))
                else:
                    act.wait_ge(sem("shift"), w.at("shift", i + 1))
                if sink_h is not None:
                    nc.scalar.activation(es, nm, ACT.Exp, bias=sink[:, sink_h:sink_h + 1])
                for t in range(T):
                    cols = (t + 1) * P if causal else S
                    src = prob[:, i % PROBS, t, 0:cols] if scale is None else ps[:, i % 2, t * S:t * S + cols]
                    last = nc.scalar.activation(prob[:, i % PROBS, t, 0:cols], src, ACT.Exp, bias=nm[:, t:t + 1],
                                                scale=scale or (-1.0 if causal else 1.0),
                                                accum_out=sm[:, t:t + 1])
                last.then_inc(sem("expd" if scale is None else "score_read_a"), 1)

            def probs_turned(sc, tn, causal):
                act.wait_ge(sem("turn_done"), w.at("turn_done", tn + 1))
                bank = ps[:, 2 + tn % 2, :].rearrange("p (k n) -> p k n", k=T)
                if causal:
                    nc.scalar.activation(probT[:, sc % 2, 0, :], bank[:, 0, :], ACT.Copy)
                    nc.scalar.activation(probT[:, sc % 2, 1, P:S], bank[:, 1, P:S], ACT.Copy)\
                        .then_inc(sem("turn_read_a"), 1)
                else:
                    nc.scalar.activation(probT[:, sc % 2, :, :], bank, ACT.Copy).then_inc(sem("turn_read_a"), 1)

            def pair_hi(pair, dst):
                act.wait_ge(sem("pair_done"), w.at("pair_done", pair + 1))
                nc.scalar.activation(dst, ps[:, 5 + 2 * (pair % 2), 0:S], ACT.Copy).then_inc(sem("pair_hi"), 1)

            def layer1():
                turned_rows_hi(TN_MIX, (1,))
                split(1)
                for t in range(T):
                    act.wait_ge(sem("half_read_v"), w.at("half_read_v", HF_Z + t + 1))
                    square(2 + 2 * t, zs[:, t, 0:Q_LORA])
                    square(3 + 2 * t, zs[:, t, Q_LORA:LORA])
                split(3)
                for t in range(T):
                    turned_hi(TN_C + t, co_hi[:, :, t * P:(t + 1) * P])
                split(2)
                cols = H1 * QK // 2
                for j in range(2):
                    for t in range(T):
                        half_there(HF_UQ + 2 * j + t)
                        nc.scalar.activation(h[:, t * 2 * cols + j * cols:t * 2 * cols + (j + 1) * cols],
                                             half_bank(HF_UQ + 2 * j + t)[:, 0:cols], ACT.Copy)\
                            .then_inc(sem("half_read_a"), 1)
                    if j == 0:
                        split(1)
                for t in range(T):
                    turned_copy(TN_QC + t, qcT[:, :, t * P:(t + 1) * P])
                for t in range(T):
                    half_there(HF_UKV + t)
                    kv = half_bank(HF_UKV + t, 2).rearrange("p (h c) -> p h c", h=H1)
                    nc.scalar.activation(kfull[:, t, :, 0:NOPE], kv[:, :, 0:NOPE], ACT.Copy)
                    nc.scalar.activation(v1[:, t, :, :], kv[:, :, NOPE:NOPE + VD], ACT.Copy)\
                        .then_inc(sem("half_read_a"), 1)

                def width_hi(g):
                    for t in range(T):
                        hf = HF_F + 3 * g + t
                        half_there(hf)
                        nc.scalar.activation(fa_hi[:, t, :], half_bank(hf), ACT.Copy).then_inc(sem("half_hi"), 1)

                def tokens_hi(g):
                    hf = HF_F + 3 * g + 2
                    half_there(hf)
                    nc.scalar.activation(four_hi[:, 2 * g:2 * g + 2, :],
                                         half_bank(hf).rearrange("p (j c) -> p j c", j=2), ACT.Copy)\
                        .then_inc(sem("half_hi"), 1)

                width_hi(0)
                for t in range(T):
                    for g in range(2):
                        turned_copy(TN_Q + 2 * t + g, qT[0:QK, 4 * g:4 * g + 4, t * P:(t + 1) * P], 4, QK)
                heads = 2 * H1

                def head_exps(i):
                    if i < H1:
                        exps(i, scale=float(QK) ** -0.5)
                    elif i < heads:
                        exps(i, sink_h=i - H1)

                def other(x):
                    if x < 2 * FGROUPS - 1:
                        if x % 2:
                            width_hi((x + 1) // 2)
                        else:
                            tokens_hi(x // 2)
                        return
                    x -= 2 * FGROUPS - 1
                    if x != 7:
                        split(1)
                    if x in (1, 3):
                        for t in range(T):
                            half_there(HF_GB + x - 1 + t)
                            n0 = x // 2 * (D // 2)
                            nc.scalar.activation(gate[:, t, n0:n0 + D // 2], half_bank(HF_GB + x - 1 + t),
                                                 ACT.Sigmoid).then_inc(sem("half_read_a"), 1)

                head_exps(0)
                other(0)
                for s in range(heads + 1):
                    head_exps(s + 1)
                    if s >= 1 and s % 2 == 0:
                        pair = (s - 1) // 2
                        pair_hi(pair, (co_hi if pair < H1 // 2 else oc_hi)[:, pair % (H1 // 2), :])
                    if s < heads:
                        probs_turned(s, TN_HEAD + s, False)
                        if s + 1 < heads:
                            other(s + 1)
                    if s in (1, 3):
                        split(1)
                split(1)
                for gate_hf, before in ((HF_GA, ("half_read_v", 6 + 12 + 4)), (HF_GC, ("merged", 2))):
                    split(2)
                    for t in range(T):
                        half_there(gate_hf + t)
                        act.wait_ge(sem(before[0]), w.at(before[0], before[1] - 1 + t))
                        nc.scalar.activation(gate[:, t, :], half_bank(gate_hf + t, 2), ACT.Sigmoid)\
                            .then_inc(sem("half_read_a"), 1)
                        split(1)
                    if gate_hf != HF_GC:
                        split(2)
                for t in range(T):
                    turned_hi(TN_P + t, hid_hi[:, :, t * P:(t + 1) * P], PLE // P)
                split(1)
                turned_rows_hi(TN_MERGE, (0,))
                split(1)
                turned_rows_hi(TN_MERGE, (1,))
                split(2)

                def copy_proj(t):
                    half_there(HF_PROJ + t)
                    nc.scalar.activation(gate[:, t, :], half_bank(HF_PROJ + t, 2), ACT.Copy)\
                        .then_inc(sem("half_read_a"), 1)

                def square_half(n, hf):
                    half_there(hf)
                    square(n, half_bank(hf, 2))

                def square_x(n, t, ready):
                    act.wait_ge(sem("x_ready"), w.at("x_ready", ready))
                    square(n, xs[:, t, :])

                square_half(6, HF_OUT)
                split(1)
                square_half(7, HF_OUT + 1)
                square_x(8, 0, 1)
                copy_proj(0)
                split(1)
                square_x(9, 1, 2)
                turned_rows_hi(TN_FFN, (0,))
                copy_proj(1)
                split(1)
                turned_rows_hi(TN_FFN, (1,))
                ffn(0, TN_HID, 0)
                square_half(10, HF_DOWN)
                square_half(11, HF_DOWN + 1)
                turned_rows_hi(TN_PLE, (0,))
                split(1)
                turned_rows_hi(TN_PLE, (1,))
                split(2)

                def gate_e(t):
                    half_there(HF_PG + t)
                    nc.scalar.activation(ht[:, t, :], half_bank(HF_PG + t, 2), ACT.Sigmoid)\
                        .then_inc(sem("half_read_a"), 1)

                def square_e(n, t):
                    act.wait_ge(sem("e_ready"), w.at("e_ready", t + 1))
                    square(n, ht[:, t, :])

                gate_e(0)
                square_e(12, 0)
                split(1)
                gate_e(1)
                square_x(13, 0, 5)
                square_e(14, 1)
                turned_rows_hi(len(TURN1) + TN_MIX, (0,))
                square_x(15, 1, 6)
                split(1)

            act.dma_start(posk[:, :], A["positions"][0:1, :].partition_broadcast(P).rearrange("p a n -> p (a n)")).then_inc(s_in["pos"], 16)
            for t in range(T):
                act.dma_start(posq[:, t:t + 1], A["positions"][0, t * P:(t + 1) * P].rearrange("(p a) -> p a", a=1))\
                    .then_inc(s_in["pos"], 16)
            act.dma_start(freq[:, :], A["freq1"][0:1, :].partition_broadcast(P).rearrange("p a n -> p (a n)")).then_inc(s_in["pos"], 16)
            act.dma_start(cs2[:, :, :, :], A["trig2"][:, :, :].rearrange("c (t p) n -> p c t n", p=P)).then_inc(s_in["const"], 16)
            act.wait_ge(s_in["x"], 16)
            at_start = True
            w.layer = 0
            for t in range(T):
                square(t, xs[:, t, :])
            split(1)
            turned_rows_hi(TN_MIX, (0,))
            split(2)
            act.wait_ge(s_setup, ANGLE_STEPS)
            nc.scalar.activation(cs1[:, :, :, :], cs1[:, :, :, :], ACT.Sin).then_inc(s_trig, 1)
            at_start = False
            with act.Fori(0, DEPTH) as li:
                w.layer = li
                done[0] = SLOTS
                layer1()
                assert done[0] == UNITS1 + SLOTS, done
            w.layer = None
            done[0] = SLOTS

            sq, tn, hf, gu, hv = T, 0, 0, 0, 0

            def square_tile(ready, t):
                act.wait_ge(sem("half_read_v"), w.at("half_read_v", ready + t + 1))
                square(sq + t, xs[:, t, :])

            def next_rows(early=0, again=False):
                nonlocal sq, tn
                square_tile(hv - T, 0)
                split(early)
                turned_rows_hi(tn, (0,))
                square_tile(hv - T, 1)
                split(1)
                turned_rows_hi(tn, (1,))
                sq, tn = sq + T, tn + 4
                if again:
                    for t in range(T):
                        square_tile(hv - T, t)
                    sq += T

            def ffn_here():
                nonlocal tn, hf, gu, hv
                ffn(gu, tn, 0)
                tn, hf, gu, hv = tn + 2 * NCH, hf + T, gu + 2 * NCH, hv + T

            def copy_out(dst, early=None, between=None, late=False):
                nonlocal hf
                split(1)
                if early is not None:
                    early()
                split(1)
                for t in range(T):
                    if t == 1 and between is not None:
                        between()
                    half_there(hf + t)
                    nc.scalar.activation(dst[:, t, :], half_bank(hf + t, 2), ACT.Copy)\
                        .then_inc(sem("half_read_a"), 1)
                    if between is None and (t == 0 or not late):
                        split(1)
                hf += T

            def turn_queries():
                nonlocal tn
                for t in range(T):
                    for g in range(2):
                        turned_copy(tn + 2 * t + g, qT2[:, 4 * g:4 * g + 4, t * P:(t + 1) * P])
                tn += 4

            def attend(sc, first=0):
                nonlocal tn
                for s in range(first, H2 + 2):
                    if s < H2:
                        exps(sc + s, causal=True)
                    if s >= 2 and s % 2:
                        pair = (s - 2) // 2
                        pair_hi((sc // 2) + pair, o2_hi[:, pair, :])
                    if 1 <= s <= H2:
                        probs_turned(sc + s - 1, tn + s - 1, True)
                tn += H2

            turned_rows_hi(tn, (1,))
            tn += 4
            ffn_here()
            next_rows()
            copy_out(q2)
            copy_out(k2, early=turn_queries)
            tn += 4

            def first_head():
                exps(0, causal=True)
                split(1)

            copy_out(v2, between=first_head)
            attend(0, 1)
            split(3)
            hf, hv = hf + T, hv + T
            next_rows(early=1)
            ffn_here()
            next_rows(again=True)
            copy_out(k2)
            copy_out(v2, late=True)
            turned_rows_hi(tn, (0,))
            split(1)
            turned_rows_hi(tn, (1,))
            tn += 4
            ffn_here()
            next_rows()
            tn += 4
            copy_out(q2)
            turn_queries()
            attend(H2)
            split(2)
            hf, hv = hf + T, hv + T
            next_rows(early=1)
            ffn_here()
            for t in range(T):
                square_tile(hv - T, t)

        @blk.vector
        def _(dve):
            w = Place()
            done = [0]
            links = [0]

            def link(ins):
                ins.then_inc(sem("v_link"), 1)
                links[0] += 1
                dve.wait_ge(sem("v_link"), w.at("v_link", links[0]))

            def split(n):
                for _ in range(n):
                    u = done[0]
                    if w.layer is None and u == len(ENDS2):
                        return
                    dve.wait_ge(sem("hi"), w.at("hi", u + 1))
                    words = unit_words(u) if w.layer is not None else UW
                    nc.vector.tensor_tensor(wlo[:, u % SLOTS, 0:words], raw[:, u % SLOTS, 0:words],
                                            whi[:, u % SLOTS, 0:words].bitcast(F32), ALU.subtract)\
                        .then_inc(sem("lo"), 1)
                    done[0] += 1

            def rest(dst, src, hi):
                return nc.vector.tensor_tensor(dst, src, hi.bitcast(F32), ALU.subtract)

            hi_n = [0]

            def turned_lo(k, dst, hi, n=4):
                hi_n[0] += 1
                dve.wait_ge(sem("turn_hi"), w.at("turn_hi", hi_n[0]))
                rest(dst, ps[:, 2 + k % 2, 0:n * P].rearrange("p (j c) -> p j c", j=n), hi)\
                    .then_inc(sem("turn_read_v"), 1)

            def turned_copy(k, dst, n=4, rows=P):
                dve.wait_ge(sem("turn_done"), w.at("turn_done", k + 1))
                nc.vector.tensor_copy(dst, ps[0:rows, 2 + k % 2, 0:n * P].rearrange("p (j c) -> p j c", j=n))\
                    .then_inc(sem("turn_read_v"), 1)

            def turned_rows_lo(k, t=None):
                for tt in range(T) if t is None else (t,):
                    for g in range(2):
                        at = (slice(None), slice(4 * g, 4 * g + 4), slice(tt * P, (tt + 1) * P))
                        turned_lo(k + 2 * tt + g, act_lo[at], act_hi[at])

            def half_there(hf):
                dve.wait_ge(sem("half_done"), w.at("half_done", hf + 1))

            def half_bank(hf, banks=1):
                return ps[:, 4 + 2 * (hf % 2):4 + 2 * (hf % 2) + banks, :].rearrange("p b n -> p (b n)")

            def scaled(n, g, dst, src, cols=None):
                dve.wait_ge(sem("inverse"), w.at("inverse", n + 1))
                dve.wait_ge(sem(f"gain_in{g % 2}"), w.at(f"gain_in{g % 2}", 16 * (g // 2 + 1)))
                row = gains[:, g % 2, :] if cols is None else gains[:, g % 2, cols[0]:cols[1]]
                return nc.vector.scalar_tensor_tensor(dst, src, stat[:, stat_of(w, n), 1:2], row,
                                                      ALU.mult, ALU.mult)

            def ffn(gu, tn):
                def times_up(gu, t):
                    dve.wait_ge(sem("silu"), w.at("silu", gu + t + 1))
                    nc.vector.tensor_tensor(hid[:, t, :], hid[:, t, :], ps[:, t, CH:2 * CH], ALU.mult)\
                        .then_inc(sem("gu_read_v"), 1)

                def hidden_lo(tn, tiles=range(T)):
                    for t in tiles:
                        at = (slice(None), slice(None), slice(t * P, (t + 1) * P))
                        turned_lo(tn + t, hid_lo[at], hid_hi[at], CH // P)

                def chunk(gu, tn):
                    times_up(gu, 0)
                    hidden_lo(tn)
                    split(1)
                    times_up(gu, 1)
                    split(2)

                times_up(gu, 0)
                split(1)
                times_up(gu, 1)
                split(1)
                chunk(gu + 2, tn)
                with dve.Fori(0, NCH - 3) as i:
                    w.chunk = i
                    chunk(gu + 4, tn + 2)
                w.chunk = None
                done[0] += 3 * (NCH - 4)
                hi_n[0] += T * (NCH - 4)
                gu, tn = gu + 2 * (NCH - 1), tn + 2 * (NCH - 1)
                hidden_lo(tn - T)
                times_up(gu, 0)
                hidden_lo(tn, (0,))
                split(1)
                times_up(gu, 1)
                split(1)
                hidden_lo(tn, (1,))

            def shifts(i, add=None, scale=1.0, sink_h=None, causal=False):
                mx, nm, _, _, _ = soft_of(i)
                dve.wait_ge(sem("score_done"), w.at("score_done", i + 1))
                if add is None:
                    link(nc.vector.tensor_reduce(mx, ps[:, i % 2, :].rearrange("p (t n) -> p t n", t=T),
                                                 AX.X, ALU.max))
                    nc.vector.tensor_scalar(nm, mx, -scale, None, ALU.mult).then_inc(sem("shift"), 1)
                    return
                if i >= PROBS:
                    dve.wait_ge(sem("turn_done"), w.at("turn_done", turn_of(i - PROBS) + 1))
                nc.vector.memset(nm if sink_h is not None else mx, 0.0)
                if sink_h is None:
                    for t in range(T):
                        cols = (t + 1) * P if causal else S
                        last = nc.vector.tensor_tensor_reduce(
                            out=prob[:, i % PROBS, t, 0:cols], in0=ps[:, i % 2, t * S:t * S + cols],
                            in1=add[:, t, 0:cols], scale=-scale, scalar=3e38, op0=ALU.add, op1=ALU.min,
                            accum_out=nm[:, t:t + 1])
                    last.then_inc(sem("score_read_v"), 1)
                    return
                for t in range(T):
                    cols = (t + 1) * P if causal else S
                    last = nc.vector.tensor_tensor_reduce(
                        out=prob[:, i % PROBS, t, 0:cols], in0=ps[:, i % 2, t * S:t * S + cols],
                        in1=add[:, t, 0:cols], scale=scale, scalar=-3e38, op0=ALU.add, op1=ALU.max,
                        accum_out=mx[:, t:t + 1])
                last.then_inc(sem("score_read_v"), 1)
                _, name, n = w.read("score", i)
                dve.wait_ge(sem(name), w.at(name, n))
                nc.vector.tensor_scalar(nm, mx, sink[:, sink_h:sink_h + 1], -1.0, ALU.max, ALU.mult)\
                    .then_inc(sem("shift"), 1)

            def normalise(i, ready, with_sink=False, causal=False):
                _, _, sm, rs, es = soft_of(i)
                dve.wait_ge(sem(ready[0]), w.at(*ready))
                if with_sink:
                    link(nc.vector.tensor_tensor(sm, sm, es, ALU.add))
                link(nc.vector.reciprocal(rs, sm))
                for t in range(T):
                    cols = (t + 1) * P if causal else S
                    last = nc.vector.tensor_scalar(prob[:, i % PROBS, t, 0:cols], prob[:, i % PROBS, t, 0:cols],
                                                   rs[:, t:t + 1], None, ALU.mult)
                last.then_inc(sem("probs"), 1)

            def pair_lo(pair, dst, hi):
                dve.wait_ge(sem("pair_hi"), w.at("pair_hi", pair + 1))
                rest(dst, ps[:, 5 + 2 * (pair % 2), 0:S], hi).then_inc(sem("pair_read_v"), 1)

            def residual(n, g, hf, t):
                scaled(n, g, ht[:, t, :], half_bank(hf, 2)).then_inc(sem("half_read_v"), 1)
                _, name, k = w.read("half", hf)
                dve.wait_ge(sem(name), w.at(name, k))
                nc.vector.tensor_tensor(xs[:, t, :], xs[:, t, :], ht[:, t, :], ALU.add)\
                    .then_inc(sem("x_ready"), 1)

            def norm_x(n, g, t, ready):
                dve.wait_ge(sem("x_ready"), w.at("x_ready", ready))
                scaled(n, g, ht[:, t, :], xs[:, t, :]).then_inc(sem("h_ready"), 1)

            def layer1():
                nonlocal half_hi
                half_hi = 0
                turned_rows_lo(TN_MIX, 1)

                def z_half(c, t):
                    hf = HF_Z + 2 * c + t
                    n0, cols = Z_CUTS[c], Z_CUTS[c + 1] - Z_CUTS[c]
                    half_there(hf)
                    nc.vector.tensor_copy(zs[:, t, n0:n0 + cols], half_bank(hf)[:, 0:cols])\
                        .then_inc(sem("half_read_v"), 1)

                z_half(0, 0)
                split(1)
                z_half(0, 1)
                for t in range(T):
                    scaled(2 + 2 * t, 1, zs[:, t, 0:Q_LORA], zs[:, t, 0:Q_LORA], (0, Q_LORA))
                    scaled(3 + 2 * t, 1, zs[:, t, Q_LORA:LORA], zs[:, t, Q_LORA:LORA], (Q_LORA, LORA))\
                        .then_inc(sem("c_ready"), 1)
                split(1)
                z_half(1, 0)
                split(1)
                z_half(1, 1)
                split(1)
                z_half(2, 0)
                for t in range(T):
                    at = (slice(None), slice(None), slice(t * P, (t + 1) * P))
                    turned_lo(TN_C + t, co_lo[at], co_hi[at])
                split(1)
                z_half(2, 1)
                split(2)
                for t in range(T):
                    turned_copy(TN_KC + t, kcT[:, :, t * P:(t + 1) * P], 2)

                def width_lo(g):
                    nonlocal half_hi
                    for t in range(T):
                        half_hi += 1
                        dve.wait_ge(sem("half_hi"), w.at("half_hi", half_hi))
                        rest(fa_lo[:, t, :], half_bank(HF_F + 3 * g + t), fa_hi[:, t, :])\
                            .then_inc(sem("half_read_v"), 1)

                def tokens_lo(g):
                    nonlocal half_hi
                    half_hi += 1
                    dve.wait_ge(sem("half_hi"), w.at("half_hi", half_hi))
                    rest(four_lo[:, 2 * g:2 * g + 2, :],
                         half_bank(HF_F + 3 * g + 2).rearrange("p (j c) -> p j c", j=2),
                         four_hi[:, 2 * g:2 * g + 2, :]).then_inc(sem("half_read_v"), 1)

                width_lo(0)
                for t in range(T):
                    for g in range(2):
                        turned_copy(TN_K + 2 * t + g, kT[0:QK, 4 * g:4 * g + 4, t * P:(t + 1) * P], 4, QK)
                heads = 2 * H1

                def head_shifts(i):
                    if i < H1:
                        shifts(i, scale=float(QK) ** -0.5)
                    elif i < heads:
                        if i == H1:
                            dve.wait_ge(sem("aux_in"), w.at("aux_in", 16))
                        dve.wait_ge(sem("alibi"), w.at("alibi", i - H1 + 1))
                        shifts(i, add=alibi[:, i % 2], scale=float(G_HD) ** -0.5, sink_h=i - H1)
                    if i < heads:
                        normalise(i, ("score_read_a", i + 1) if i < H1 else ("expd", i - H1 + 1), i >= H1)

                def other(x):
                    if x < 2 * FGROUPS - 1:
                        if x % 2:
                            width_lo((x + 1) // 2)
                        else:
                            tokens_lo(x // 2)
                        return
                    x -= 2 * FGROUPS - 1
                    for c, t in {5: ((0, 0), (0, 1)), 7: ((1, 0),), 8: ((1, 1),)}.get(x, ()):
                        hf = HF_BB + 2 * c + t
                        half_there(hf)
                        n0 = c * (D // 2)
                        times_gate(ht, t, n0, n0 + D // 2, HF_GB + 2 * c + t, half_bank(hf))
                    if x == 0:
                        done[0] += 2
                        dve.wait_ge(sem("lo"), w.at("lo", done[0]))
                    if x != 7:
                        split(1)

                def times_gate(dst, t, n0, n1, gate_hf, src):
                    _, name, k = w.read("half", gate_hf)
                    dve.wait_ge(sem(name), w.at(name, k))
                    nc.vector.tensor_tensor(dst[:, t, n0:n1], gate[:, t, n0:n1], src, ALU.mult)\
                        .then_inc(sem("half_read_v"), 1)

                head_shifts(0)
                other(0)
                for s in range(heads + 1):
                    head_shifts(s + 1)
                    if s >= 1 and s % 2 == 0:
                        pair = (s - 1) // 2
                        k = pair % (H1 // 2)
                        hi, lo = (co_hi, co_lo) if pair < H1 // 2 else (oc_hi, oc_lo)
                        pair_lo(pair, lo[:, k, :], hi[:, k, :])
                    if s + 1 < heads:
                        other(s + 1)
                split(1)
                def add_branch(t, gate_hf, hf, ready):
                    half_there(hf)
                    times_gate(gate, t, 0, D, gate_hf, half_bank(hf, 2))
                    _, name, k = w.read("half", hf)
                    dve.wait_ge(sem(name), w.at(name, k))
                    nc.vector.tensor_tensor(ht[:, t, :], ht[:, t, :], gate[:, t, :], ALU.add)\
                        .then_inc(sem(ready), 1)

                split(4)
                for t in range(T):
                    add_branch(t, HF_GA + t, HF_BA + t, "merged")
                    split(1)
                split(4)
                for t in range(T):
                    at = (slice(None), slice(None), slice(t * P, (t + 1) * P))
                    turned_lo(TN_P + t, hid_lo[at], hid_hi[at], PLE // P)
                add_branch(0, HF_GC, HF_BC, "h_ready")
                turned_rows_lo(TN_MERGE, 0)
                split(1)
                add_branch(1, HF_GC + 1, HF_BC + 1, "h_ready")
                turned_rows_lo(TN_MERGE, 1)
                split(3)
                residual(6, 2, HF_OUT, 0)
                split(1)
                residual(7, 2, HF_OUT + 1, 1)
                norm_x(8, 3, 0, 1)
                turned_rows_lo(TN_FFN, 0)
                split(1)
                norm_x(9, 3, 1, 2)
                split(1)
                turned_rows_lo(TN_FFN, 1)
                ffn(0, TN_HID)
                residual(10, 4, HF_DOWN, 0)
                turned_rows_lo(TN_PLE, 0)
                split(1)
                residual(11, 4, HF_DOWN + 1, 1)
                split(1)
                turned_rows_lo(TN_PLE, 1)
                split(2)

                def embed(t):
                    _, name, k = w.read("half", HF_PG + t)
                    dve.wait_ge(sem(name), w.at(name, k))
                    nc.vector.tensor_tensor(ht[:, t, :], ht[:, t, :], gate[:, t, :], ALU.mult)\
                        .then_inc(sem("e_ready"), 1)

                def add_embedded(n, t):
                    link(scaled(n, 5, ht[:, t, :], ht[:, t, :]))
                    nc.vector.tensor_tensor(xs[:, t, :], xs[:, t, :], ht[:, t, :], ALU.add)\
                        .then_inc(sem("x_ready"), 1)

                embed(0)
                add_embedded(12, 0)
                embed(1)
                norm_x(13, 6, 0, 5)
                link(scaled(14, 5, ht[:, 1, :], ht[:, 1, :]))
                turned_rows_lo(len(TURN1) + TN_MIX, 0)
                nc.vector.tensor_tensor(xs[:, 1, :], xs[:, 1, :], ht[:, 1, :], ALU.add)\
                    .then_inc(sem("x_ready"), 1)
                split(1)
                norm_x(15, 6, 1, 6)
                split(1)

            def turn_of(i):
                return TN_HEAD + i if w.layer is not None else head_turns[i]

            half_hi = 0
            w.layer = 0
            for t in range(T):
                scaled(t, 0, ht[:, t, :], xs[:, t, :]).then_inc(sem("h_ready"), 1)
            split(1)
            turned_rows_lo(TN_MIX, 0)
            split(2)
            n_parts = [0]

            def parts(ins):
                ins.then_inc(s_parts, 1)
                n_parts[0] += 1

            dve.wait_ge(s_in["pos"], 64)
            for src, dst in ((posk[:, :], ki), (posq[:, :], posi)):
                parts(nc.vector.tensor_scalar(dst[:, 0, :], src, 12, None, ALU.arith_shift_right))
                parts(nc.vector.tensor_scalar(dst[:, 1, :], src, 4095, None, ALU.bitwise_and))
            dve.wait_ge(s_parts, n_parts[0])
            parts(nc.vector.tensor_copy(kf, ki))
            parts(nc.vector.tensor_copy(posf[:, 1:3, :], posi[:, :, :]))
            assert n_parts[0] == PART_STEPS
            dve.wait_ge(s_parts, n_parts[0])
            parts(nc.vector.tensor_scalar(mask[:, 0, :], kf[:, 0, :], posf[:, 1, 0:1], 4096.0,
                                          ALU.subtract, ALU.mult))
            parts(nc.vector.tensor_scalar(df[:, 0, :], kf[:, 1, :], posf[:, 2, 0:1], None, ALU.subtract))
            dve.wait_ge(s_parts, n_parts[0])
            parts(nc.vector.tensor_tensor(df[:, 0, :], df[:, 0, :], mask[:, 0, :], ALU.add))
            dve.wait_ge(s_parts, n_parts[0])
            parts(nc.vector.scalar_tensor_tensor(mask[:, 0, :], df[:, 0, :], -1.0, df[:, 0, :],
                                                 ALU.mult, ALU.max))
            assert n_parts[0] == DISTANCE_STEPS
            with dve.Fori(0, DEPTH) as li:
                w.layer = li
                done[0], links[0], hi_n[0] = SLOTS, 0, T
                layer1()
                assert done[0] == UNITS1 + SLOTS, done
                assert links[0] == PER_LAYER["v_link"], links
                assert hi_n[0] == PER_LAYER["turn_hi"] + T, hi_n
            w.layer = None
            done[0], links[0], hi_n[0] = SLOTS, 0, T

            n, tn, hf, gu = T, 0, 0, 0
            head_turns = {}

            def norm_tile(t):
                scaled(n + t, n // 2, ht[:, t, :], xs[:, t, :]).then_inc(sem("h_ready"), 1)

            def add_tile(t, scale):
                half_there(hf + t)
                if scale is None:
                    nc.vector.tensor_tensor(xs[:, t, :], xs[:, t, :], half_bank(hf + t, 2), ALU.add)\
                        .then_inc(sem("half_read_v"), 1)
                else:
                    nc.vector.scalar_tensor_tensor(xs[:, t, :], half_bank(hf + t, 2), scale, xs[:, t, :],
                                                   ALU.mult, ALU.add).then_inc(sem("half_read_v"), 1)

            def add_and_norm(scale=None):
                nonlocal n, tn, hf
                add_tile(0, scale)
                norm_tile(0)
                add_tile(1, scale)
                turned_rows_lo(tn, 0)
                split(1)
                norm_tile(1)
                split(1)
                turned_rows_lo(tn, 1)
                n, tn, hf = n + T, tn + 4, hf + T

            def ffn_here():
                nonlocal tn, gu
                ffn(gu, tn)
                tn, gu = tn + 2 * NCH, gu + 2 * NCH

            def turn_keys():
                nonlocal tn
                for t in range(T):
                    for g in range(2):
                        turned_copy(tn + 2 * t + g, kT2[:, 4 * g:4 * g + 4, t * P:(t + 1) * P])
                tn += 4

            def attend(sc, mask_n, early=0):
                nonlocal tn
                dve.wait_ge(s_in["mask"], 16 * mask_n)
                for i in range(H2):
                    head_turns[sc + i] = tn + i
                for s in range(H2 + 3):
                    if s < H2:
                        shifts(sc + s, add=mask, scale=float(HD2) ** -0.5, causal=True)
                    if s >= 4 and s % 2 == 0:
                        pair = (s - 3) // 2
                        pair_lo(sc // 2 + pair, o2_lo[:, pair, :], o2_hi[:, pair, :])
                    if s == 0:
                        split(early)
                    if 1 <= s <= H2:
                        normalise(sc + s - 1, ("expd", sc + s), causal=True)
                tn += H2

            turned_rows_lo(tn, 1)
            tn += 4
            ffn_here()
            add_and_norm(0.5)
            split(9)
            hf += 3 * T
            tn += 4
            turn_keys()
            split(1)
            attend(0, 1, early=1)
            split(3)
            add_and_norm()
            ffn_here()
            add_and_norm(0.5)
            split(4)
            for t in range(T):
                norm_tile(t)
            split(3)
            hf += 2 * T
            turned_rows_lo(tn, 0)
            split(1)
            turned_rows_lo(tn, 1)
            n, tn = n + T, tn + 4
            ffn_here()
            add_and_norm(0.5)
            split(2)
            turn_keys()
            split(2)
            hf += T
            tn += 4
            attend(H2, 2)
            split(2)
            add_and_norm()
            ffn_here()
            for t in range(T):
                add_tile(t, 0.5)
                scaled(n + t, n // 2, ht[:, t, :], xs[:, t, :]).then_inc(sem("result"), 1)

        @blk.gpsimd
        def _(pool):
            w = Place()
            links = [0]

            def link(ins):
                ins.then_inc(sem("g_link"), 1)
                links[0] += 1
                pool.wait_ge(sem("g_link"), w.at("g_link", links[0]))

            def inverse(n):
                pool.wait_ge(sem("squared"), w.at("squared", n + 1))
                c = stat_of(w, n)
                link(nc.gpsimd.tensor_tensor(stat[:, c, 1:2], stat[:, c, 0:1], eps[:, :], ALU.add))
                nc.gpsimd.tensor_tensor(stat[:, c, 1:2], stat[:, c, 1:2], half_pow[:, :], ALU.pow)\
                    .then_inc(sem("inverse"), 1)

            def load_gain(row, slot, after=None):
                if after is not None:
                    pool.wait_ge(sem(after[0]), w.at(*after))
                pool.dma_start(gains[:, slot, :], A["gains"][bass.ds(row, 1), :].partition_broadcast(P)
                               .rearrange("p a n -> p (a n)")).then_inc(sem(f"gain_in{slot}"), 16)

            def rotate(src, dst, c, s, n_heads, half, ready):
                tiles = src[0].shape[1]
                words = tiles * n_heads * half
                flat = alibi[:, :, :, :].rearrange("p a t n -> p (a t n)")
                prod = [flat[:, k * words:(k + 1) * words].rearrange("p (t h c) -> p t h c", t=tiles, h=n_heads)
                        for k in range(4)]
                shape = [P, tiles, n_heads, half]
                cb = c.unsqueeze(2).to_broadcast(shape)
                sb_ = s.unsqueeze(2).to_broadcast(shape)
                for k, (x, y) in enumerate(((src[0], cb), (src[1], sb_), (src[0], sb_), (src[1], cb))):
                    last = nc.gpsimd.tensor_tensor(prod[k], x, y, ALU.mult)
                link(last)
                a, b, c_, d = prod
                if dst[0].shape[2] != n_heads:
                    a, b, c_, d = (q.to_broadcast(list(dst[0].shape)) for q in prod)
                for t in range(tiles):
                    nc.gpsimd.tensor_tensor(dst[0][:, t], a[:, t], b[:, t], ALU.subtract)
                    last = nc.gpsimd.tensor_tensor(dst[1][:, t], c_[:, t], d[:, t], ALU.add)
                last.then_inc(sem(ready), 1)

            def layer1(li):
                for t in range(T):
                    inverse(2 + 2 * t)
                    inverse(3 + 2 * t)
                pool.wait_ge(sem("pair_done"), w.at("pair_done", 0))
                pool.dma_start(sink[:, :], A["gqa_sink"][bass.ds(li, 1), :].partition_broadcast(P)
                               .rearrange("p a n -> p (a n)")).then_inc(sem("aux_in"), 16)
                load_gain(li * 6 + 2, 0, ("h_ready", 2))
                pool.wait_ge(sem("half_read_v"), w.at("half_read_v", HF_Z + 6))
                load_gain(li * 6 + 3, 1, ("c_ready", 2))
                nc.gpsimd.tensor_copy(vc[:, :, :], zs[:, :, Z_VC:Z_SMALL])
                nc.gpsimd.tensor_copy(kswap[:, :, 0:G_HD], zs[:, :, Z_KC + G_HD:Z_VC])
                nc.gpsimd.tensor_copy(kswap[:, :, G_HD:2 * G_HD], zs[:, :, Z_KC:Z_KC + G_HD])\
                    .then_inc(sem("kc_ready"), 1)
                r = ROPE // 2
                zr = zs[:, :, LORA:LORA + ROPE].unsqueeze(2)
                pool.wait_ge(sem("half_read_a"), w.at("half_read_a", 4))
                halves = (hq[:, :, :, NOPE:NOPE + r], hq[:, :, :, NOPE + r:QK])
                rotate(halves, halves, cs1[:, 0], cs1[:, 1], H1, r, "q_ready")
                pool.wait_ge(sem("q_ready"), w.at("q_ready", 1))
                rotate((zr[:, :, :, 0:r], zr[:, :, :, r:ROPE]),
                       (kfull[:, :, :, NOPE:NOPE + r], kfull[:, :, :, NOPE + r:QK]),
                       cs1[:, 0], cs1[:, 1], 1, r, "k_ready")
                pool.wait_ge(sem("k_ready"), w.at("k_ready", 1))
                for i in range(H1):
                    if i >= 2:
                        pool.wait_ge(sem("score_read_v"), w.at("score_read_v", i - 1))
                    nc.gpsimd.tensor_tensor(alibi[:, i % 2], mask[:, :, :],
                                            slopes[:, i:i + 1].unsqueeze(2).to_broadcast([P, T, S]),
                                            ALU.mult).then_inc(sem("alibi"), 1)
                    if i == 1:
                        for u in (U_GATE_B, U_GATE_B + 1):
                            pool.wait_ge(sem("lo"), w.at("lo", u))
                            pool.wait_ge(sem("hi"), w.at("hi", u + 1))
                            nc.gpsimd.tensor_tensor(wlo[:, u % SLOTS, :], raw[:, u % SLOTS, :],
                                                    whi[:, u % SLOTS, :].bitcast(F32), ALU.subtract)\
                                .then_inc(sem("lo"), 1)
                pool.wait_ge(sem("pair_done"), w.at("pair_done", H1))
                pool.dma_start(probT[:, 0, :, :], A["p"][bass.ds(li, 1), 0, :, :]
                               .rearrange("a (t p) n -> p (a t) n", p=P)).then_inc(sem("aux_in"), 16)
                for n in range(6, 10):
                    inverse(n)
                load_gain(li * 6 + 4, 0, ("x_ready", 2))
                load_gain(li * 6 + 5, 1, ("h_ready", 6))
                for n in range(10, 12):
                    inverse(n)
                load_gain(li * 6 + 6, 0, ("x_ready", 4))
                for n in range(12, 16):
                    inverse(n)
                load_gain(li * 6 + 7, 1, ("x_ready", 6))

            n_setup = [0]

            def setup(ins):
                ins.then_inc(s_setup_g, 1)
                n_setup[0] += 1
                pool.wait_ge(s_setup_g, n_setup[0])

            nc.gpsimd.memset(half_pow[:, :], -0.5)
            nc.gpsimd.memset(eps[:, :], EPS)
            for i in range(H1):
                last = nc.gpsimd.memset(slopes[:, i:i + 1], -2.0 ** (-8.0 * (i + 1) / H1) * float(G_HD) ** 0.5)
            last.then_inc(s_ident, 1)
            setup(nc.gpsimd.memset(ident[:, :], 0.0))
            nc.gpsimd.affine_select(out=ident[:, :], in_=ident[:, :], compare_op=ALU.not_equal, fill=1.0,
                                    base=0, pattern=[[-1, P]], channel_multiplier=1).then_inc(s_ident, 1)
            load_gain(0, 0)
            load_gain(1, 1)
            pool.wait_ge(s_ident, 2)
            w.layer = 0
            for t in range(T):
                inverse(t)
            n_table = [0]

            def table(ins):
                ins.then_inc(s_setup, 1)
                n_table[0] += 1
                pool.wait_ge(s_setup, n_table[0])

            pool.wait_ge(s_in["pos"], 64)
            words = T * (ROPE // 2)
            angle, turns_, near, whole = (hid[:, 0, n * words:(n + 1) * words].rearrange("p (t f) -> p t f", t=T)
                                   for n in range(4))
            table(nc.gpsimd.tensor_copy(posf[:, 0, :], posq[:, :]))
            for t in range(T):
                table(nc.gpsimd.tensor_scalar(angle[:, t, :], freq[:, :], posf[:, 0, t:t + 1], None, ALU.mult))
            two_pi = 2 * math.pi
            part1 = 6.28125
            part2 = float(np.float32(math.floor((two_pi - part1) * 2.0 ** 21) / 2.0 ** 21))
            part3 = float(np.float32(two_pi - part1 - part2))
            magic = 1.5 * 2.0 ** 23
            for which in range(2):
                quarter = 0.25 if which == 0 else 0.0
                table(nc.gpsimd.tensor_scalar(turns_, angle, 1.0 / two_pi, quarter, ALU.mult, ALU.add))
                table(nc.gpsimd.tensor_scalar(turns_, turns_, magic, None, ALU.add))
                table(nc.gpsimd.tensor_scalar(turns_, turns_, magic, None, ALU.subtract))
                src = angle
                for part in (part1, part2, part3):
                    table(nc.gpsimd.tensor_scalar(whole, turns_, -part, None, ALU.mult))
                    table(nc.gpsimd.tensor_tensor(near, whole, src, ALU.add))
                    src = near
                table(nc.gpsimd.tensor_scalar(near, near, quarter * two_pi, 3.141592, ALU.add, ALU.min))
                table(nc.gpsimd.tensor_scalar(cs1[:, which], near, -3.141592, None, ALU.max))
            assert n_table[0] == ANGLE_STEPS
            pool.wait_ge(s_parts, PART_STEPS)
            table(nc.gpsimd.tensor_scalar(mask[:, 1, :], kf[:, 0, :], posf[:, 1, 1:2], 4096.0,
                                          ALU.subtract, ALU.mult))
            table(nc.gpsimd.tensor_scalar(df[:, 1, :], kf[:, 1, :], posf[:, 2, 1:2], None, ALU.subtract))
            table(nc.gpsimd.tensor_tensor(df[:, 1, :], df[:, 1, :], mask[:, 1, :], ALU.add))
            table(nc.gpsimd.tensor_scalar(mask[:, 1, :], df[:, 1, :], 0.0, None, ALU.min))
            table(nc.gpsimd.tensor_scalar(df[:, 1, :], df[:, 1, :], 0.0, None, ALU.max))
            table(nc.gpsimd.tensor_tensor(mask[:, 1, :], df[:, 1, :], mask[:, 1, :], ALU.subtract))
            assert n_table[0] == SETUP_STEPS
            pool.wait_ge(s_parts, DISTANCE_STEPS)
            setup(nc.gpsimd.affine_select(out=mask[:, 0, :], in_=mask[:, 0, :], compare_op=ALU.is_ge, fill=BIG,
                                          base=P, pattern=[[-1, S]], channel_multiplier=1))
            setup(nc.gpsimd.affine_select(out=mask[:, 1, :], in_=mask[:, 1, :], compare_op=ALU.is_ge, fill=BIG,
                                          base=0, pattern=[[1, S]], channel_multiplier=-1))
            pool.wait_ge(s_trig, 1)
            with pool.Fori(0, DEPTH) as li:
                w.layer = li
                links[0] = T
                layer1(li)
                assert links[0] == PER_LAYER["g_link"] + T, links
            w.layer = None
            links[0] = T

            n = T
            first_row = 6 * DEPTH

            def norm_here():
                nonlocal n
                for t in range(T):
                    inverse(n + t)
                n += T
                if n // 2 + 1 < 8:
                    load_gain(first_row + n // 2 + 1, (n // 2 + 1) % 2, ("h_ready", n))

            def rotate_heads(buf, ready, after, n_ready):
                v = buf[:, :, :].rearrange("p t (h c) -> p t h c", h=H2)
                for t in range(T):
                    one = slice(t, t + 1)
                    pool.wait_ge(sem("half_read_a"), w.at("half_read_a", after - T + t + 1))
                    halves = (v[:, one, :, 0:ROT // 2], v[:, one, :, ROT // 2:ROT])
                    rotate(halves, halves, cs2[:, 0, one], cs2[:, 1, one], H2, ROT // 2, ready)
                    pool.wait_ge(sem(ready), w.at(ready, T * (n_ready - 1) + t + 1))

            def load_mask(k):
                pool.dma_start(mask[:, :, :], A["masks"][k, :, :].rearrange("(t p) n -> p t n", p=P))\
                    .then_inc(s_in["mask"], 16)

            pool.wait_ge(s_in["const"], 16)
            pool.wait_ge(sem("alibi"), w.at("alibi", 0))
            load_mask(0)
            load_gain(first_row + 2, 0, ("h_ready", 2))
            norm_here()
            rotate_heads(q2, "q_ready", 2, 1)
            rotate_heads(k2, "k_ready", 4, 1)
            norm_here()
            load_mask(1)
            norm_here()
            rotate_heads(k2, "k_ready", 8, 2)
            norm_here()
            norm_here()
            rotate_heads(q2, "q_ready", 12, 2)
            norm_here()
            norm_here()


def host_constants():
    i = np.arange(S)
    angle = 2 * np.pi * (np.outer(i, i) % S) / S
    c, s = np.cos(angle) / 16.0, np.sin(angle) / 16.0
    dft = np.concatenate([c, -s, s], axis=1).astype(np.float32)
    half = ROPE // 2
    freq1 = (np.float32(THETA1) ** (-np.arange(half, dtype=np.float32) / np.float32(half)))
    freq1 = freq1.astype(np.float32).reshape(1, half)
    half = ROT // 2
    freq2 = (np.float32(THETA2) ** (-np.arange(half, dtype=np.float32) / np.float32(half))).astype(np.float32)
    ang2 = (np.arange(S, dtype=np.float32)[:, None] * freq2[None, :]).astype(np.float64)
    trig2 = np.stack([np.cos(ang2), np.sin(ang2)]).astype(np.float32)
    back = i[:, None] - i[None, :]
    count = np.zeros((S, S))
    for window, step in WINDOWS:
        count += (back >= 0) & (back <= window) & (back % step == 0)
    first = np.where(count > 0, np.log(np.maximum(count, 1)) * HD2 ** 0.5, -BIG)
    second = np.where(back >= 0, 0.0, -BIG)
    masks = np.stack([first, second]).astype(np.float32)
    return dict(dft=dft, freq1=freq1, trig2=trig2, masks=masks)


_WEIGHTS = ("w_in", "w_uq", "w_ukv", "w_branch_a", "w_branch_b", "w_branch_c", "w_out", "w_ffn_gate",
            "w_ffn_up", "w_ffn_down", "w_ple_proj", "w_ple_gate", "ffn1_w_gate_2", "ffn1_w_up_2",
            "ffn1_w_down_2", "ffn2_w_gate_2", "ffn2_w_up_2", "ffn2_w_down_2", "a_w_qkv_2", "a_w_o_2",
            "kv_w_2", "b_w_q_2", "b_w_o_2")


def device_arrays(inputs):
    arrays = {n: np.ascontiguousarray(inputs[n]) for n in ("x", "p", "positions", "gqa_sink", *_WEIGHTS)}
    rows = []
    for i in range(DEPTH):
        latent = np.zeros(D, np.float32)
        latent[0:Q_LORA] = inputs["mla_q_norm"][i]
        latent[Q_LORA:LORA] = inputs["mla_kv_norm"][i]
        rows += [inputs["norm_mix_pre"][i], latent, inputs["norm_mix_post"][i], inputs["norm_ffn_pre"][i],
                 inputs["norm_ffn_post"][i], inputs["norm_ple"][i]]
    for i in range(DEPTH):
        rows += [inputs["ffn1_norm_2"][i], inputs["mix_norm_2"][i], inputs["ffn2_norm_2"][i]]
        if i == 0:
            rows.append(inputs["kv_norm_2"])
    rows.append(inputs["final_norm_2"])
    arrays["gains"] = np.stack([np.asarray(r, np.float32) for r in rows])
    arrays.update(host_constants())
    return arrays


def kernel(**inputs):
    import concourse.bacc as bacc
    from concourse.bass_utils import run_bass_kernel_spmd

    nc = bacc.Bacc("TRN2", target_bir_lowering=False, num_devices=1)
    arrays = device_arrays({k: np.asarray(v) for k, v in inputs.items()})
    aps = {n: nc.dram_tensor(n + "_dram", a.shape, mybir.dt.from_np(a.dtype), kind="ExternalInput").ap()
           for n, a in arrays.items()}
    out = nc.dram_tensor("out_dram", (1, S, D), F32, kind="ExternalOutput").ap()
    two_blocks(nc, aps, out)
    result = run_bass_kernel_spmd(nc, [{n + "_dram": a for n, a in arrays.items()}], core_ids=[0])
    return result.results[0]["out_dram"]
```
